# Optimizing a Trainium2 kernel written in Bass

```python
import math
import jax, jax.numpy as jnp
from jax import lax
import numpy as np

D_MODEL = 1024
BATCH = 1
SEQ = 512
DEPTH = 1

HEAD_DIM = 64
N_HEADS_TOTAL = D_MODEL // HEAD_DIM
A_HEADS = N_HEADS_TOTAL // 4
B_HEADS = 3 * N_HEADS_TOTAL // 8
C_HEADS = N_HEADS_TOTAL - A_HEADS - B_HEADS
C_KV_HEADS = 2
C_GROUP = C_HEADS // C_KV_HEADS
A_QK_DIM = HEAD_DIM // 2
A_V_DIM = HEAD_DIM
MOBA_BLOCK = 256
MOBA_TOPK = 3
MOBA_QCHUNK = 32
WINDOW = 128
DENSE_QBLOCK = 128
ALIBI_MAX = 8.0
A_Q_W = A_HEADS * 2 * A_QK_DIM
A_K_W = A_HEADS * 2 * A_QK_DIM
A_V_W = A_HEADS * A_V_DIM
B_W = B_HEADS * HEAD_DIM
C_Q_W = C_HEADS * HEAD_DIM
C_KV_W = C_KV_HEADS * HEAD_DIM
IN_WIDTH = A_Q_W + A_K_W + A_V_W + 3 * B_W + C_Q_W + 2 * C_KV_W
MIX_WIDTH = A_V_W + B_W + C_Q_W
PEER_HEADS = 8
PEER_NKEYS = 128
PEER_N = PEER_NKEYS * PEER_NKEYS
PEER_TOPK = 16
PEER_QDIM = 256
PEER_CHUNK = 128
N_MOD = 6
EPS = 1e-6

kernel_name = "hymba_diff_moba_swa_peer_adaln"

def rmsnorm(x, g):
    xf = x.astype(jnp.float32)
    y = xf * lax.rsqrt(jnp.mean(xf * xf, axis=-1, keepdims=True) + EPS)
    return (y * g.astype(jnp.float32)).astype(x.dtype)

def alibi_slopes():
    n = N_HEADS_TOTAL
    return 2.0 ** (-ALIBI_MAX * jnp.arange(1, n + 1, dtype=jnp.float32) / n)

def diff_attention(q, k, v, slopes, lam, lam_init, subln_g):
    B, S, H, _, dk = q.shape
    nq = S // DENSE_QBLOCK
    scale = dk ** -0.5
    pos_k = jnp.arange(S, dtype=jnp.float32)
    qb = q.reshape(B, nq, DENSE_QBLOCK, H, 2, dk).transpose(1, 0, 2, 3, 4, 5)

    def block(args):
        i, qi = args
        pos_q = (i * DENSE_QBLOCK + jnp.arange(DENSE_QBLOCK)).astype(jnp.float32)
        dist = pos_q[:, None] - pos_k[None, :]
        s = jnp.einsum('bqhmd,bshmd->bhmqs', qi, k).astype(jnp.float32) * scale
        s = jnp.where((dist >= 0)[None, None, None],
                      s - slopes[None, :, None, None, None] * dist[None, None, None], -jnp.inf)
        p = jax.nn.softmax(s, axis=-1)
        w = (p[:, :, 0] - lam * p[:, :, 1]).astype(v.dtype)
        return jnp.einsum('bhqs,bshd->bqhd', w, v)

    o = lax.map(block, (jnp.arange(nq), qb))
    o = o.transpose(1, 0, 2, 3, 4).reshape(B, S, H, -1)
    return rmsnorm(o, subln_g) * (1.0 - lam_init)

def moba_attention(q, k, v, slopes):
    B, S, H, d = q.shape
    L = MOBA_BLOCK
    nb = -(-S // L)
    Sp = nb * L
    pad = ((0, 0), (0, Sp - S), (0, 0), (0, 0))
    q = jnp.pad(q, pad)
    k = jnp.pad(k, pad)
    v = jnp.pad(v, pad)
    K = min(MOBA_TOPK, nb)
    nc = Sp // MOBA_QCHUNK
    scale = d ** -0.5
    kbh = k.reshape(B, nb, L, H, d).transpose(0, 3, 1, 2, 4)
    vbh = v.reshape(B, nb, L, H, d).transpose(0, 3, 1, 2, 4)
    kmean = jnp.mean(kbh.astype(jnp.float32), axis=3)
    gate = jnp.einsum('bshd,bhnd->bshn', q.astype(jnp.float32), kmean)
    q_blk = jnp.arange(Sp) // L
    past = jnp.arange(nb)[None, :] < q_blk[:, None]
    gate = jnp.where(past[None, :, None, :], gate, -jnp.inf)
    gsc, sel = lax.top_k(gate, K)
    valid = jnp.isfinite(gsc)
    b_idx = jnp.arange(B)[:, None, None, None]
    h_idx = jnp.arange(H)[None, None, :, None]
    offs = jnp.arange(L)
    KL = K * L

    def chunk(i):
        t0 = i * MOBA_QCHUNK
        qc = lax.dynamic_slice_in_dim(q, t0, MOBA_QCHUNK, axis=1)
        selc = lax.dynamic_slice_in_dim(sel, t0, MOBA_QCHUNK, axis=1)
        valc = lax.dynamic_slice_in_dim(valid, t0, MOBA_QCHUNK, axis=1)
        pos_q = (t0 + jnp.arange(MOBA_QCHUNK)).astype(jnp.float32)
        k_sel = kbh[b_idx, h_idx, selc]
        v_sel = vbh[b_idx, h_idx, selc]
        own = t0 // L
        k_own = lax.dynamic_index_in_dim(kbh, own, axis=2, keepdims=False)
        v_own = lax.dynamic_index_in_dim(vbh, own, axis=2, keepdims=False)
        s_sel = jnp.einsum('bqhd,bqhkld->bqhkl', qc, k_sel).astype(jnp.float32) * scale
        pos_sel = (selc[..., None] * L + offs).astype(jnp.float32)
        dist_sel = pos_q[None, :, None, None, None] - pos_sel
        s_sel = jnp.where(valc[..., None], s_sel - slopes[:, None, None] * dist_sel, -jnp.inf)
        pos_own = (own * L + offs).astype(jnp.float32)
        dist_own = pos_q[:, None] - pos_own[None, :]
        s_own = jnp.einsum('bqhd,bhld->bqhl', qc, k_own).astype(jnp.float32) * scale
        s_own = jnp.where((dist_own >= 0)[None, :, None, :],
                          s_own - slopes[:, None] * dist_own[None, :, None, :], -jnp.inf)
        s_all = jnp.concatenate([s_sel.reshape(B, MOBA_QCHUNK, H, KL), s_own], axis=-1)
        p = jax.nn.softmax(s_all, axis=-1).astype(v.dtype)
        p_sel = p[..., :KL].reshape(B, MOBA_QCHUNK, H, K, L)
        p_own = p[..., KL:]
        return (jnp.einsum('bqhkl,bqhkld->bqhd', p_sel, v_sel)
                + jnp.einsum('bqhl,bhld->bqhd', p_own, v_own))

    o = lax.map(chunk, jnp.arange(nc))
    return o.transpose(1, 0, 2, 3, 4).reshape(B, Sp, H, d)[:, :S]

def swa_sink_attention(q, k, v, slopes, sinks):
    B, S, Hq, d = q.shape
    W = WINDOW
    nb = S // W
    scale = d ** -0.5
    qb = q.reshape(B, nb, W, C_KV_HEADS, C_GROUP, d)

    def with_prev(t):
        tb = t.reshape(B, nb, W, C_KV_HEADS, d)
        prev = jnp.pad(tb, ((0, 0), (1, 0), (0, 0), (0, 0), (0, 0)))[:, :-1]
        return jnp.concatenate([prev, tb], axis=2)

    kb = with_prev(k)
    vb = with_prev(v)
    s = jnp.einsum('bnqhgd,bnkhd->bnhgqk', qb, kb).astype(jnp.float32) * scale
    qq = jnp.arange(W)
    kk = jnp.arange(2 * W)
    rel = (qq[:, None] + W - kk[None, :]).astype(jnp.float32)
    key_pos = jnp.arange(nb)[:, None] * W - W + kk[None, :]
    mask = (rel >= 0)[None] & (rel < W)[None] & (key_pos >= 0)[:, None, :]
    sl = slopes.reshape(C_KV_HEADS, C_GROUP)
    s = jnp.where(mask[None, :, None, None], s - sl[:, :, None, None] * rel, -jnp.inf)
    sink = jnp.broadcast_to(sinks.astype(jnp.float32).reshape(C_KV_HEADS, C_GROUP)[None, None, :, :, None, None],
                            s.shape[:-1] + (1,))
    p = jax.nn.softmax(jnp.concatenate([s, sink], axis=-1), axis=-1)[..., :-1].astype(v.dtype)
    o = jnp.einsum('bnhgqk,bnkhd->bnqhgd', p, vb)
    return o.reshape(B, S, Hq, d)

def mixer(h, w_in, w_out, lam, lam_init, subln_g, sinks):
    B, S, _ = h.shape
    proj = jnp.einsum('bsd,de->bse', h, w_in)
    cuts = np.cumsum([A_Q_W, A_K_W, A_V_W, B_W, B_W, B_W, C_Q_W, C_KV_W]).tolist()
    qa, ka, va, qb, kb, vb, qc, kc, vc = jnp.split(proj, cuts, axis=-1)
    slopes = alibi_slopes()
    sl_c = slopes[:C_HEADS]
    sl_a = slopes[C_HEADS:C_HEADS + A_HEADS]
    sl_b = slopes[C_HEADS + A_HEADS:]
    oa = diff_attention(qa.reshape(B, S, A_HEADS, 2, A_QK_DIM), ka.reshape(B, S, A_HEADS, 2, A_QK_DIM),
                        va.reshape(B, S, A_HEADS, A_V_DIM), sl_a, lam, lam_init, subln_g)
    ob = moba_attention(qb.reshape(B, S, B_HEADS, HEAD_DIM), kb.reshape(B, S, B_HEADS, HEAD_DIM),
                        vb.reshape(B, S, B_HEADS, HEAD_DIM), sl_b)
    oc = swa_sink_attention(qc.reshape(B, S, C_HEADS, HEAD_DIM), kc.reshape(B, S, C_KV_HEADS, HEAD_DIM),
                            vc.reshape(B, S, C_KV_HEADS, HEAD_DIM), sl_c, sinks)
    o = jnp.concatenate([oa.reshape(B, S, A_V_W), ob.reshape(B, S, B_W), oc.reshape(B, S, C_Q_W)], axis=-1)
    return jnp.einsum('bse,ed->bsd', o, w_out)

def peer_ffn(h, wq, sub_keys, u, v):
    B, S, D = h.shape
    T = B * S
    xs = h.reshape(T // PEER_CHUNK, PEER_CHUNK, D)

    def chunk(xc):
        q = jnp.einsum('td,de->te', xc, wq).reshape(PEER_CHUNK, PEER_HEADS, 2, PEER_QDIM // 2)
        s = jnp.einsum('thpd,hpnd->thpn', q, sub_keys).astype(jnp.float32)
        sv, si = lax.top_k(s, PEER_TOPK)
        cand = (sv[:, :, 0, :, None] + sv[:, :, 1, None, :]).reshape(PEER_CHUNK, PEER_HEADS, -1)
        cidx = (si[:, :, 0, :, None] * PEER_NKEYS + si[:, :, 1, None, :]).reshape(PEER_CHUNK, PEER_HEADS, -1)
        top, pos = lax.top_k(cand, PEER_TOPK)
        eidx = jnp.take_along_axis(cidx, pos, axis=-1)
        g = jax.nn.softmax(top, axis=-1)
        ue = u[eidx]
        ve = v[eidx]
        a = jax.nn.gelu(jnp.einsum('thkd,td->thk', ue, xc).astype(jnp.float32), approximate=False)
        return jnp.einsum('thk,thkd->td', (g * a).astype(ve.dtype), ve)

    return lax.map(chunk, xs).reshape(B, S, D)

def setup_inputs(seed: int = 0) -> dict:
    key = jax.random.key(seed)
    ks = jax.random.split(key, 20)
    f32 = jnp.float32
    D = D_MODEL

    def nrm(k, shape, scale):
        return jax.random.normal(k, shape, f32) * scale

    return {
        "x": nrm(ks[0], (BATCH, SEQ, D), 1.0),
        "c": nrm(ks[1], (BATCH, D), 1.0),
        "norm1_g": 1.0 + nrm(ks[2], (DEPTH, D), 0.02),
        "norm2_g": 1.0 + nrm(ks[3], (DEPTH, D), 0.02),
        "w_ada": nrm(ks[4], (DEPTH, D, N_MOD * D), 0.5 * D ** -0.5),
        "b_ada": nrm(ks[5], (DEPTH, N_MOD * D), 0.02),
        "w_in": nrm(ks[6], (DEPTH, D, IN_WIDTH), D ** -0.5),
        "w_out": nrm(ks[7], (DEPTH, MIX_WIDTH, D), MIX_WIDTH ** -0.5),
        "lam_q1": nrm(ks[8], (DEPTH, A_QK_DIM), 0.1),
        "lam_k1": nrm(ks[9], (DEPTH, A_QK_DIM), 0.1),
        "lam_q2": nrm(ks[10], (DEPTH, A_QK_DIM), 0.1),
        "lam_k2": nrm(ks[11], (DEPTH, A_QK_DIM), 0.1),
        "subln_g": 1.0 + nrm(ks[12], (DEPTH, A_V_DIM), 0.02),
        "sinks": nrm(ks[13], (DEPTH, C_HEADS), 0.5),
        "peer_wq": nrm(ks[14], (DEPTH, D, PEER_HEADS * PEER_QDIM), D ** -0.5),
        "peer_keys": nrm(ks[15], (DEPTH, PEER_HEADS, 2, PEER_NKEYS, PEER_QDIM // 2), (PEER_QDIM // 2) ** -0.5),
        "peer_u": nrm(ks[16], (DEPTH, PEER_N, D), D ** -0.5),
        "peer_v": nrm(ks[17], (DEPTH, PEER_N, D), (PEER_HEADS * PEER_TOPK) ** -0.5),
        "final_g": 1.0 + nrm(ks[18], (D,), 0.02),
    }

def reference(x, c, norm1_g, norm2_g, w_ada, b_ada, w_in, w_out, lam_q1, lam_k1, lam_q2, lam_k2,
              subln_g, sinks, peer_wq, peer_keys, peer_u, peer_v, final_g):
    cs = jax.nn.silu(c)
    for l in range(DEPTH):
        mod = jnp.einsum('bd,de->be', cs, w_ada[l]) + b_ada[l]
        sh1, sc1, g1, sh2, sc2, g2 = [m[:, None, :] for m in jnp.split(mod, N_MOD, axis=-1)]
        lam_init = 0.8 - 0.6 * math.exp(-0.3 * l)
        lam = (jnp.exp(jnp.sum(lam_q1[l].astype(jnp.float32) * lam_k1[l].astype(jnp.float32)))
               - jnp.exp(jnp.sum(lam_q2[l].astype(jnp.float32) * lam_k2[l].astype(jnp.float32))) + lam_init)
        h = rmsnorm(x, norm1_g[l]) * (1.0 + sc1) + sh1
        x = x + g1 * mixer(h, w_in[l], w_out[l], lam, lam_init, subln_g[l], sinks[l])
        h = rmsnorm(x, norm2_g[l]) * (1.0 + sc2) + sh2
        x = x + g2 * peer_ffn(h, peer_wq[l], peer_keys[l], peer_u[l], peer_v[l])
    return rmsnorm(x, final_g)


_drawn_inputs = setup_inputs


def setup_inputs(seed=0):
    import zlib

    import numpy as np

    out = dict(_drawn_inputs(seed))
    spreads = {}
    factors = {'norm1_g': 8.0,
     'norm2_g': 8.0,
     'b_ada': 3.997,
     'lam_q1': 64.0,
     'lam_k1': 64.0,
     'lam_q2': 6.187,
     'lam_k2': 8.0,
     'subln_g': 8.0,
     'sinks': 64.0,
     'peer_wq': 3.691,
     'peer_keys': 3.719,
     'peer_u': 4.102,
     'peer_v': 3.717,
     'final_g': 8.142}
    for name, (base, spread) in spreads.items():
        noise = np.random.default_rng([zlib.crc32(name.encode()), seed]).standard_normal(out[name].shape)
        drawn = base * np.exp(spread * noise) if base else spread * noise
        out[name] = __import__('jax').numpy.asarray(drawn.astype(out[name].dtype))
    for name, factor in factors.items():
        out[name] = (out[name] * factor).astype(out[name].dtype)
    return out
```

```python
import numpy as np
import concourse.bass as bass
from concourse import mybir
from contextlib import ExitStack

P = 128
D, S = 1024, 512
KD = D // P
NT = S // P
HD = 64
NA, NB, NCH = 4, 6, 6
CG = NCH // 2
NHEADS = NA + NB + NCH
QK_TILES, V_COLS = 14, 768
IN_TILES = QK_TILES + V_COLS // P
PH, TOPK, NKEYS = 8, 16, 128
EPS = 1e-6
LAM_INIT = 0.8 - 0.6
MASKED = -1e30
SLOPES = [2.0 ** (-8.0 * n / NHEADS) for n in range(1, NHEADS + 1)]


def head_plan():
    plan = []
    for h in range(NA):
        maps = [(h // 2, 2 + h // 2, 64 * (h % 2) + 32 * m, 32) for m in range(2)]
        plan.append(("A", maps, 32 ** -0.5, SLOPES[NCH + h], h * HD, None))
    for h in range(NB):
        plan.append(("B", [(4 + h // 2, 7 + h // 2, 64 * (h % 2), 64)], 64 ** -0.5,
                     SLOPES[NCH + NA + h], 256 + h * HD, None))
    for h in range(NCH):
        kv = h // CG
        plan.append(("C", [(10 + h % CG, 13, 64 * kv, 64)], 64 ** -0.5, SLOPES[h], 640 + kv * HD, h))
    return plan


def peer_block_kernel(nc, x, c_col, norm1_col, w_ada, b_ada, w_in, w_out, lam_vecs, subln_row, sinks_row,
                      norm2_row, wq, keys_t, peer_u, peer_v, final_row, out):
    f32, u32 = mybir.dt.float32, mybir.dt.uint32
    ALU, ACT, AX = mybir.AluOpType, mybir.ActivationFunctionType, mybir.AxisListType.X
    ctx = ExitStack()
    with ctx:
        def sb(name, shape, dt=f32):
            return ctx.enter_context(nc.sbuf_tensor(name, shape, dt))

        def sem(name):
            return ctx.enter_context(nc.semaphore(name))

        x_sb = sb("x_sb", [P, NT, D])
        h2 = sb("h2", [P, NT, D])
        hT = sb("hT", [P, KD, S])
        qkT = sb("qkT", [P, QK_TILES, S])
        v_sb = sb("v_sb", [P, NT, V_COLS])
        ring_w = sb("ring_w", [P, 8, D])
        ring_a = sb("ring_a", [P, 8, D])
        keys = sb("keys", [P, 2 * PH, NKEYS])
        g1_row = sb("g1_row", [P, D])
        a2_row = sb("a2_row", [P, D])
        sh2_row = sb("sh2_row", [P, D])
        g2_row = sb("g2_row", [P, D])
        ident = sb("ident", [P, P])
        ones = sb("ones", [P, P])
        ndist = sb("ndist", [P, S])
        ndist_w = sb("ndist_w", [P, 2 * P])
        mod_acc = sb("mod_acc", [P, 2, 512])
        b_half = sb("b_half", [1, 2, 512])
        c_in = sb("c_in", [P, KD])
        c_silu = sb("c_silu", [P, KD])
        c_tmp = sb("c_tmp", [P, KD])
        n1_col = sb("n1_col", [P, KD])
        a1_col = sb("a1_col", [P, KD])
        sh1_col = sb("sh1_col", [P, KD])
        lam_in = sb("lam_in", [P, 4, 32])
        lam_prod = sb("lam_prod", [P, 2, 32])
        lam_s = sb("lam_s", [P, 8])
        subln = sb("subln", [P, HD])
        sinks = sb("sinks", [P, NCH])
        nsinks = sb("nsinks", [P, NCH])
        ss = sb("ss", [P, 3 * NT])
        rstd = sb("rstd", [P, 3 * NT])
        MAPS = NA + NHEADS
        mx = sb("mx", [P, NT * MAPS])
        nmax = sb("nmax", [P, NT * MAPS])
        den = sb("den", [P, NT * MAPS])
        esink = sb("esink", [P, NT * NCH])
        rden = sb("rden", [P, NT, NHEADS])
        ra = sb("ra", [P, NT * NA, 2])
        sso = sb("sso", [P, NT, NA, 2])
        si = sb("si", [P, NT, PH, 2, TOPK], u32)
        topp = sb("topp", [P, NT, PH, TOPK], u32)
        rep = mod_acc[:, 0, :]
        cand = mod_acc[:, 1, :].rearrange("p (h a b) -> p h a b", a=TOPK, b=TOPK)
        side_u = sb("side_u", [P, 2, PH * TOPK], u32)
        eidx = sb("eidx", [P, NT, PH * TOPK], u32)
        gate = sb("gate", [P, NT, PH * TOPK])
        gsum = sb("gsum", [P, PH])
        iota16 = sb("iota16", [P, TOPK])
        stage = sb("stage", [P, 2, TOPK], u32)
        dots = sb("dots", [P, TOPK])
        act_g = sb("act_g", [P, TOPK])
        wgt = sb("wgt", [P, TOPK])
        late = v_sb[:, :, :].rearrange("p t c -> p (t c)")
        sv = late[:, 0:1024].rearrange("p (t h s k) -> p t h s k", t=NT, h=PH, s=2)
        topv = late[:, 1024:1536].rearrange("p (t h k) -> p t h k", t=NT, h=PH)
        sif = late[:, 1536:1792].rearrange("p (h s k) -> p h s k", h=PH, s=2)
        side_f = late[:, 1792:2048].rearrange("p (s k) -> p s k", s=2)
        key_f = late[:, 2048:2304].rearrange("p (s k) -> p s k", s=2)
        xn = qkT[:, 0:8, :].rearrange("p (t a) s -> p t (a s)", t=NT)
        Sb = hT[:, 0:4, :]
        pT = hT[:, 4:6, :]
        oT = hT[:, 6, :].rearrange("p (a b) -> p a b", b=P), hT[:, 7, :].rearrange("p (a b) -> p a b", b=P)
        o_sb = sb("o_sb", [P, D])
        junk = o_sb
        w_outs = ring_w
        onehot = ring_w[:, 0:2, :].rearrange("p a b -> p (a b)")
        sc = qkT[:, 0:8, :]
        qT = qkT[:, 8:11, :]
        y = qkT[:, 0:8, :].rearrange("p (t a) s -> p t (a s)", t=NT)
        ring = [ring_a[:, j, :] for j in range(8)] + [ring_w[:, j, :] for j in range(8)]

        bank = {n: ctx.enter_context(nc.psum_tensor("bank_" + n, [P, 512], f32))
                for n in ("S0", "S1", "S2", "T0", "T1", "O0", "O1", "G")}
        full = {n: sem("full_" + n) for n in bank}
        free = {n: sem("free_" + n) for n in bank}
        turn = {}
        fillings = dict.fromkeys(bank, 0)

        s_x, s_out = sem("x_loaded"), sem("out_stored")
        s_c, s_n1, s_lam, s_small = sem("c_loaded"), sem("norm1_loaded"), sem("lam_loaded"), sem("rows_loaded")
        s_ada = [sem("ada_loaded0"), sem("ada_loaded1")]
        s_win = [sem(f"w_loaded{j}") for j in range(8)]
        s_wout, s_keys, s_fin = sem("w_out_loaded"), sem("keys_loaded"), sem("final_loaded")
        s_wq = [sem(f"wq_loaded{j}") for j in range(8)]
        s_const = sem("constants_made")
        s_accd, s_modu, s_rows = sem("mod_summed"), sem("mod_used"), sem("mod_rows_ready")
        s_winu, s_wqu = sem("w_in_used"), sem("wq_used")
        s_dv, s_ac = sem("vector_steps"), sem("scalar_steps")
        s_ce, s_ss, s_ms, s_std, s_xn = sem("exp_c"), sem("squares"), sem("mean_squares"), sem("std"), sem("xn_ready")
        s_a1, s_hT, s_qk, s_v = sem("mod_cols_ready"), sem("hT_ready"), sem("qk_ready"), sem("v_ready")
        s_lp, s_le = sem("lam_sums"), sem("lam_exps")
        s_nm, s_exp, s_es, s_comb = sem("nmax_ready"), sem("exp_done"), sem("sink_exp"), sem("probs_ready")
        s_pt, s_pTr, s_pv = sem("probs_transposed"), sem("pT_ready"), sem("pv_done")
        s_sso, s_so, s_o, s_oTr, s_y = sem("o_squares"), sem("o_std"), sem("o_ready"), sem("oT_ready"), sem("oproj_done")
        s_x1, s_h2, s_h2T = sem("x1_ready"), sem("h2_ready"), sem("h2T_ready")
        s_qT, s_qTu, s_sc, s_scu = sem("qT_ready"), sem("qT_used"), sem("scores_ready"), sem("scores_used")
        s_gd, s_ge, s_idx = sem("gate_shifted"), sem("gate_exp"), sem("experts_ready")
        s_got = [sem(f"row_got{j}") for j in range(16)]
        s_used, s_stg, s_gel, s_w = sem("rows_used"), sem("staged"), sem("gelu_done"), sem("weights_ready")
        s_clear = sem("slots_cleared")
        s_x2, s_f2, s_fs, s_res = sem("x2_ready"), sem("x2_squares"), sem("x2_std"), sem("result_ready")

        tally = {}

        def done(eng, ins, s):
            tally[s.name] = tally.get(s.name, 0) + 1
            ins.then_inc(s, 1)
            eng.wait_ge(s, tally[s.name])

        plan = head_plan()
        JOBS = [(i, j) for i in range(NT) for j in range(NHEADS)]
        first_map = []
        for i, j in JOBS:
            first_map.append(i * MAPS + sum(len(plan[a][1]) for a in range(j)))
        ADA_ORDER = [1, 0, 2, 4, 3, 5]
        ADA_HALVES = [(s, b) for s in ADA_ORDER for b in range(2)]

        N = len(JOBS)

        def key_tiles(i, j):
            return range(max(0, i - 1), i + 1) if plan[j][0] == "C" else range(i + 1)

        block = ctx.enter_context(nc.Block())

        @block.tensor
        def _(pe):
            def take(b, key):
                if fillings[b]:
                    pe.wait_ge(free[b], fillings[b])
                fillings[b] += 1
                turn[key] = (b, fillings[b])
                return bank[b]

            def emptied(key):
                b, n = turn[key]
                pe.wait_ge(free[b], n)

            pe.wait_ge(s_const, 5)
            cols = take("G", "mod_cols")
            for n in range(4):
                pe.wait_ge(s_accd, n + 1)
                for m in range(4):
                    at = n * 4 + m
                    pe.matmul(cols[:, at:at + 1], mod_acc[:, n % 2, m * P:m * P + P], ones[:, 0:1],
                              start=True, stop=False)
                    mm = pe.matmul(cols[:, at:at + 1], b_half[0:1, n % 2, m * P:m * P + P], ones[0:1, 0:1],
                                   start=False, stop=True)
                mm.then_inc(full["G"] if n == 3 else s_modu, 1)
            for k in range(KD):
                b = f"T{k % 2}"
                ps = take(b, ("xT", k))
                for i in range(NT):
                    if k == 0:
                        pe.wait_ge(s_xn, i + 1)
                    mm = pe.transpose(ps[:, i * P:i * P + P], xn[:, i, k * P:k * P + P], ident[:, :])
                mm.then_inc(full[b], 1)

            def mod_row(n):
                ps = take("G", ("row", n))
                pe.wait_ge(s_accd, n + 1)
                pe.matmul(ps[:, :], ones[:, :], mod_acc[:, n % 2, :], start=True, stop=False)
                pe.matmul(ps[:, :], ones[0:1, :], b_half[0:1, n % 2, :], start=False, stop=True)\
                    .then_inc(full["G"], 1)

            for e in range(QK_TILES):
                b = f"S{e % 3}"
                ps = take(b, ("qk", e))
                pe.wait_ge(s_win[e % 8], 16 * (e // 8 + 1))
                for k in range(KD):
                    if e == 0:
                        emptied(("xT", k))
                    mm = pe.matmul(ps[:, :], ring_w[:, e % 8, k * P:k * P + P], hT[:, k, :],
                                   start=(k == 0), stop=(k == KD - 1))
                mm.then_inc(full[b], 1)
                if 2 <= e < 10:
                    mod_row(e + 2)
            for n in range(V_COLS // 256):
                e = QK_TILES + 2 * n
                for a in (e, e + 1):
                    pe.wait_ge(s_win[a % 8], 16 * (a // 8 + 1))
                w = ring_w[:, e % 8:e % 8 + 2, :].rearrange("p a (k c) -> p a k c", k=KD)
                for i in range(NT):
                    b = f"O{i % 2}"
                    ps = take(b, ("v", n, i))
                    for k in range(KD):
                        mm = pe.matmul(ps[:, 0:256], hT[:, k, i * P:i * P + P], w[:, :, k, :],
                                       start=(k == 0), stop=(k == KD - 1))
                    mm.then_inc(full[b], 1)

            for e in range(QK_TILES - 3, QK_TILES):
                emptied(("qk", e))
            maps_done = [0]

            def scores(J):
                i, j = JOBS[J]
                kt = key_tiles(i, j)
                for m, (qt, kk, part, rows) in enumerate(plan[j][1]):
                    b = f"S{maps_done[0] % 3}"
                    maps_done[0] += 1
                    ps = take(b, ("s", first_map[J] + m))
                    pe.matmul(ps[:, 0:len(kt) * P], qkT[part:part + rows, qt, i * P:i * P + P],
                              qkT[part:part + rows, kk, kt[0] * P:(kt[-1] + 1) * P],
                              start=True, stop=True).then_inc(full[b], 1)

            def transpose_probs(J):
                i, j = JOBS[J]
                b = f"T{J % 2}"
                ps = take(b, ("pT", J))
                if plan[j][0] == "A":
                    pe.wait_ge(s_comb, i * NA + j + 1)
                else:
                    pe.wait_ge(s_exp, first_map[J] + 1)
                for n, kt in enumerate(key_tiles(i, j)):
                    mm = pe.transpose(ps[:, n * P:n * P + P], Sb[:, first_map[J] % 4, n * P:n * P + P], ident[:, :])
                mm.then_inc(full[b], 1)

            def pv(J):
                i, j = JOBS[J]
                b = f"O{j // 8}"
                ps = take(b, ("o", i, j // 8)) if j % 8 == 0 else bank[b]
                if J == 0:
                    emptied(("v", 2, 2))
                    emptied(("v", 2, 3))
                emptied(("pT", J))
                col = plan[j][4]
                kt = key_tiles(i, j)
                for n, t in enumerate(kt):
                    mm = pe.matmul(ps[:, (j % 8) * HD:(j % 8) * HD + HD], pT[:, J % 2, n * P:n * P + P],
                                   v_sb[:, t, col:col + HD], start=(n == 0), stop=(n == len(kt) - 1))
                mm.then_inc(full[b] if j % 8 == 7 else s_pv, 1)

            def out_proj(i):
                for half in range(2):
                    b = f"T{half}"
                    ps = take(b, ("oT", i, half))
                    pe.wait_ge(s_o, i + 1)
                    for n in range(4):
                        k = half * 4 + n
                        mm = pe.transpose(ps[:, n * P:n * P + P], o_sb[:, k * P:k * P + P], ident[:, :])
                    mm.then_inc(full[b], 1)
                if i == 0:
                    pe.wait_ge(s_wout, 16)
                emptied(("oT", i, 0))
                emptied(("oT", i, 1))
                for half, b in enumerate(("G", "T0")):
                    ps = take(b, ("y", i, half))
                    for k in range(KD):
                        mm = pe.matmul(ps[:, :], oT[k // 4][:, k % 4, :],
                                       w_outs[:, k, half * 512:half * 512 + 512],
                                       start=(k == 0), stop=(k == KD - 1))
                    mm.then_inc(full[b], 1)

            scores(0)
            for J in range(N + 5):
                if J + 1 < N:
                    scores(J + 1)
                if 1 <= J <= N:
                    transpose_probs(J - 1)
                if 2 <= J < N + 2:
                    pv(J - 2)
                if J >= 5 and (J - 5) % NHEADS == NHEADS - 1:
                    out_proj((J - 5) // NHEADS)

            pe.wait_ge(s_h2, NT)
            for k in range(KD):
                b = f"T{k % 2}"
                ps = take(b, ("h2T", k))
                for i in range(NT):
                    mm = pe.transpose(ps[:, i * P:i * P + P], h2[:, i, k * P:k * P + P], ident[:, :])
                mm.then_inc(full[b], 1)
            kb = ["T0", "T1", "O0", "O1"]

            def key_scores(e):
                emptied(("q", e))
                for i in range(NT):
                    ps = take(kb[i], ("sc", e // 4, i)) if e % 4 == 0 else bank[kb[i]]
                    mm = pe.matmul(ps[:, (e % 4) * P:(e % 4) * P + P], qT[:, e % 3, i * P:i * P + P], keys[:, e, :],
                                   start=True, stop=True)
                    if e % 4 == 3:
                        mm.then_inc(full[kb[i]], 1)
                if e % 4 != 3:
                    mm.then_inc(s_qTu, 1)

            for e in range(2 * PH):
                b = f"S{e % 3}"
                ps = take(b, ("q", e))
                pe.wait_ge(s_wq[e % 8], 16 * (e // 8 + 1))
                for k in range(KD):
                    if e == 0:
                        emptied(("h2T", k))
                    mm = pe.matmul(ps[:, :], ring_a[:, e % 8, k * P:k * P + P], hT[:, k, :],
                                   start=(k == 0), stop=(k == KD - 1))
                mm.then_inc(full[b], 1)
                if e == 0:
                    pe.wait_ge(s_keys, 16)
                if e >= 1:
                    key_scores(e - 1)
            key_scores(2 * PH - 1)

        def taken(eng, key):
            b, n = turn[key]
            eng.wait_ge(full[b], n)
            return bank[b]

        def emptied(eng, key):
            b, n = turn[key]
            eng.wait_ge(free[b], n)

        def half_used(eng, n):
            if n < 3:
                eng.wait_ge(s_modu, n + 1)
            else:
                taken(eng, "mod_cols" if n == 3 else ("row", n))

        def freeing(key):
            return free[turn[key][0]]

        def pv_done(eng, J):
            i, j = JOBS[J]
            if j % 8 == 7:
                taken(eng, ("o", i, j // 8))
            else:
                eng.wait_ge(s_pv, J + 1 - (J + 1) // 8)

        def map_bufs_free(eng, m):
            if m >= 4:
                J = max(a for a in range(N) if first_map[a] <= m - 4)
                taken(eng, ("pT", J))

        @block.sync
        def _(sp):
            def ada(n):
                s, b = ADA_HALVES[n]
                if n >= 2:
                    sp.wait_ge(s_accd, n - 1)
                    half_used(sp, n - 2)
                dst = ring_a[:, 4 * (n % 2):4 * (n % 2) + 4, :].rearrange("p a b -> p (a b)")
                at = s * D + b * 512
                sp.dma_start(dst.rearrange("p (k c) -> p k c", k=KD),
                             w_ada[:, at:at + 512].rearrange("(k p) c -> p k c", p=P)).then_inc(s_ada[n % 2], 16)
                sp.dma_start(b_half[0:1, n % 2, :], b_ada[0:1, at:at + 512]).then_inc(s_ada[n % 2], 16)

            def win(e):
                if e >= 8:
                    b, n = turn[("qk", e - 8)]
                    sp.wait_ge(full[b], n)
                sp.dma_start(ring_w[:, e % 8, :], w_in[e]).then_inc(s_win[e % 8], 16)

            sp.dma_start(x_sb[:, :, :], x[0].rearrange("(t p) d -> p t d", p=P)).then_inc(s_x, 16)
            for n in range(4):
                ada(n)
            for e in range(8):
                win(e)
                if e >= 4:
                    ada(e)
            for e in range(8, IN_TILES):
                win(e)
                if e < 12:
                    ada(e)
            for i in (2, 3):
                b, n = turn[("v", 2, i)]
                sp.wait_ge(full[b], n)
            sp.dma_start(w_outs[:, :, :], w_out.rearrange("(k p) d -> p k d", p=P)).then_inc(s_wout, 16)
            sp.dma_start(keys[:, :, :], keys_t).then_inc(s_keys, 16)
            sp.wait_ge(s_accd, 12)
            for e in range(2 * PH):
                if e >= 8:
                    b, n = turn[("q", e - 8)]
                    sp.wait_ge(full[b], n)
                sp.dma_start(ring_a[:, e % 8, :], wq[e]).then_inc(s_wq[e % 8], 16)
            sp.wait_ge(s_x1, NT)
            sp.dma_start(g1_row[:, :], final_row.partition_broadcast(P)).then_inc(s_fin, 16)
            for i in range(NT):
                sp.wait_ge(s_res, i + 1)
                sp.dma_start(out[0, i * P:i * P + P, :], x_sb[:, i, :]).then_inc(s_out, 16)
            sp.wait_ge(s_out, 16 * NT)

        @block.gpsimd
        def _(pool):
            pool.memset(ident[:, :], 0.0).then_inc(s_const, 1)
            pool.memset(ones[:, :], 1.0).then_inc(s_const, 1)
            pool.iota(ndist[:, :], [[1, S]], base=-(S - P), channel_multiplier=-1,
                      allow_small_or_imprecise_dtypes=True).then_inc(s_const, 1)
            pool.iota(iota16[:, :], [[1, TOPK]], base=0, channel_multiplier=0,
                      allow_small_or_imprecise_dtypes=True).then_inc(s_const, 1)
            pool.wait_ge(s_const, 4)
            pool.affine_select(out=ident[:, :], in_=ident[:, :], compare_op=ALU.not_equal, fill=1.0, base=0,
                               pattern=[[-1, P]], channel_multiplier=1).then_inc(s_const, 1)
            pool.affine_select(out=ndist[:, :], in_=ndist[:, :], compare_op=ALU.is_ge, fill=MASKED, base=S - P,
                               pattern=[[-1, S]], channel_multiplier=1).then_inc(s_const, 1)
            pool.wait_ge(s_const, 6)
            pool.affine_select(out=ndist_w[:, :], in_=ndist[:, 2 * P:4 * P], compare_op=ALU.is_ge, fill=MASKED,
                               base=-1, pattern=[[1, 2 * P]], channel_multiplier=-1).then_inc(s_const, 1)

            def gathers(i, head, parity, reused):
                G = head + i * PH
                pool.wait_ge(s_idx, i + 1)
                if reused:
                    pool.wait_ge(s_used, 2 + 32 * (G - 1))
                    pool.sem_inc(s_clear, 1)
                pool.tensor_copy(stage[:, parity, :], eidx[:, i, bass.ds(head * TOPK, TOPK)]).then_inc(s_stg, 1)
                for table, first in ((peer_u, 0), (peer_v, TOPK)):
                    for j in range(TOPK):
                        if j == 0 and first == 0:
                            pool.wait_ge(s_stg, G + 1)
                            pool.sem_inc(s_clear, 1)
                        if reused or parity or first:
                            pool.wait_ge(s_used, 2 + 32 * G + first - TOPK + j + 1)
                            pool.sem_inc(s_clear, 1)
                        pool.indirect_dma_start(ring[j], None, table[:, :],
                                                bass.IndirectOffsetOnAxis(stage[:, parity, j:j + 1], 0))\
                            .then_inc(s_got[j], 16)

            for i in range(NT):
                if i == 0:
                    pool.wait_ge(s_idx, NT)
                    gathers(0, 0, 0, False)
                    gathers(0, 1, 1, False)
                with pool.Fori(1 if i == 0 else 0, PH // 2) as two:
                    gathers(i, 2 * two, 0, True)
                    gathers(i, 2 * two + 1, 1, True)

        @block.scalar
        def _(act):
            act.dma_start(c_in[:, :], c_col).then_inc(s_c, 16)
            act.dma_start(n1_col[:, :], norm1_col).then_inc(s_n1, 16)
            act.dma_start(lam_in[:, :, :].rearrange("p a b -> p (a b)"), lam_vecs.partition_broadcast(P))\
               .then_inc(s_lam, 16)
            act.dma_start(subln[:, :], subln_row.partition_broadcast(P)).then_inc(s_small, 16)
            act.dma_start(sinks[:, :], sinks_row.partition_broadcast(P)).then_inc(s_small, 16)
            act.dma_start(a2_row[:, :], norm2_row.partition_broadcast(P)).then_inc(s_small, 16)
            act.wait_ge(s_c, 16)
            act.activation(c_tmp[:, :], c_in[:, :], ACT.Exp, scale=-1.0).then_inc(s_ce, 1)
            act.wait_ge(s_lp, 1)
            act.activation(lam_s[:, 2:4], lam_s[:, 0:2], ACT.Exp).then_inc(s_le, 1)
            act.wait_ge(s_x, 16)
            for i in range(NT):
                act.activation(xn[:, i, :], x_sb[:, i, :], ACT.Square, accum_out=ss[:, i:i + 1]).then_inc(s_ss, 1)
            act.wait_ge(s_ms, 1)
            act.activation(rstd[:, 0:NT], ss[:, 0:NT], ACT.Sqrt).then_inc(s_std, 1)
            emptied(act, "mod_cols")
            for k in range(KD):
                ps = taken(act, ("xT", k))
                act.activation(hT[:, k, :], ps[:, :], ACT.Identity, scale=a1_col[:, k:k + 1],
                               bias=sh1_col[:, k:k + 1]).then_inc(freeing(("xT", k)), 1)
            for e in range(QK_TILES):
                ps = taken(act, ("qk", e))
                act.activation(qkT[:, e, :], ps[:, :], ACT.Copy).then_inc(freeing(("qk", e)), 1)

            def exps(J):
                i, j = JOBS[J]
                kind, maps, scale, _, _, c = plan[j]
                n = len(key_tiles(i, j)) * P
                for m in range(first_map[J], first_map[J] + len(maps)):
                    act.wait_ge(s_nm, m + 1)
                    act.activation(Sb[:, m % 4, 0:n], Sb[:, m % 4, 0:n], ACT.Exp, scale=scale,
                                   bias=nmax[:, m:m + 1], accum_out=den[:, m:m + 1]).then_inc(s_exp, 1)
                if kind == "C":
                    a = i * NCH + c
                    act.activation(esink[:, a:a + 1], sinks[:, c:c + 1], ACT.Exp,
                                   bias=nmax[:, m:m + 1]).then_inc(s_es, 1)

            def take_pT(J):
                n = len(key_tiles(*JOBS[J])) * P
                ps = taken(act, ("pT", J))
                if J >= 2:
                    pv_done(act, J - 2)
                act.activation(pT[:, J % 2, 0:n], ps[:, 0:n], ACT.Copy).then_inc(freeing(("pT", J)), 1)

            for J in range(N + 5):
                if J < N:
                    exps(J)
                if 1 <= J <= N:
                    take_pT(J - 1)
                if J >= 2 and (J - 2) % NHEADS == NHEADS - 1:
                    i = (J - 2) // NHEADS
                    act.wait_ge(s_sso, i + 1)
                    act.activation(sso[:, i, :, 1], sso[:, i, :, 0], ACT.Sqrt).then_inc(s_so, 1)
                if J >= 5 and (J - 5) % NHEADS == NHEADS - 1:
                    i = (J - 5) // NHEADS
                    for half in range(2):
                        ps = taken(act, ("oT", i, half))
                        if i >= 1 and half == 0:
                            taken(act, ("y", i - 1, 1))
                        act.activation(oT[half][:, :, :], ps[:, :].rearrange("p (a b) -> p a b", b=P),
                                       ACT.Copy).then_inc(freeing(("oT", i, half)), 1)

            act.wait_ge(s_ms, 2)
            act.activation(rstd[:, NT:2 * NT], ss[:, NT:2 * NT], ACT.Sqrt).then_inc(s_std, 1)
            for k in range(KD):
                ps = taken(act, ("h2T", k))
                act.activation(hT[:, k, :], ps[:, :], ACT.Copy).then_inc(freeing(("h2T", k)), 1)

            def take_scores(g):
                for i in range(NT):
                    ps = taken(act, ("sc", g, i))
                    n = g * NT + i
                    if n >= 8:
                        act.wait_ge(s_scu, n - 7)
                    act.activation(sc[:, n % 8, :], ps[:, :], ACT.Copy).then_inc(freeing(("sc", g, i)), 1)

            for e in range(2 * PH):
                ps = taken(act, ("q", e))
                if e >= 3:
                    last = e - 3
                    if last % 4 == 3:
                        taken(act, ("sc", last // 4, NT - 1))
                    else:
                        act.wait_ge(s_qTu, last + 1 - (last + 1) // 4)
                act.activation(qT[:, e % 3, :], ps[:, :], ACT.Copy).then_inc(freeing(("q", e)), 1)
                if e % 4 == 0 and e:
                    take_scores(e // 4 - 1)
            take_scores(3)
            for i in range(NT):
                act.wait_ge(s_gd, i + 1)
                act.activation(gate[:, i, :], gate[:, i, :], ACT.Exp).then_inc(s_ge, 1)
            for i in range(NT):
                with act.Fori(i * PH, (i + 1) * PH) as G:
                    act.wait_ge(s_used, 2 + 32 * G + TOPK)
                    act.activation(act_g[:, :], dots[:, :], ACT.Gelu).then_inc(s_gel, 1)
                act.wait_ge(s_f2, i + 1)
                act.activation(rstd[:, 2 * NT + i:2 * NT + i + 1], ss[:, 2 * NT + i:2 * NT + i + 1], ACT.Sqrt)\
                   .then_inc(s_fs, 1)

        @block.vector
        def _(dve):
            def bcast(ap, shape):
                return ap.to_broadcast(shape)

            dve.wait_ge(s_ce, 1)
            done(dve, dve.tensor_scalar(c_tmp[:, :], c_tmp[:, :], 1.0, None, ALU.add), s_dv)
            done(dve, dve.reciprocal(c_tmp[:, :], c_tmp[:, :]), s_dv)
            done(dve, dve.tensor_tensor(c_silu[:, :], c_in[:, :], c_tmp[:, :], ALU.mult), s_dv)
            dve.wait_ge(s_lam, 16)
            done(dve, dve.tensor_tensor(lam_prod[:, :, :], lam_in[:, 0:4:2, :], lam_in[:, 1:4:2, :], ALU.mult), s_dv)
            dve.tensor_reduce(lam_s[:, 0:2], lam_prod[:, :, :], AX, ALU.add).then_inc(s_lp, 1)
            dve.wait_ge(s_le, 1)
            done(dve, dve.tensor_tensor(lam_s[:, 4:5], lam_s[:, 3:4], lam_s[:, 2:3], ALU.subtract), s_dv)
            done(dve, dve.tensor_scalar(lam_s[:, 5:6], lam_s[:, 4:5], -LAM_INIT, None, ALU.add), s_dv)
            dve.wait_ge(s_small, 48)
            done(dve, dve.tensor_scalar(subln[:, :], subln[:, :], 1.0 - LAM_INIT, None, ALU.mult), s_dv)
            done(dve, dve.tensor_scalar(nsinks[:, :], sinks[:, :], -1.0, None, ALU.mult), s_dv)
            dve.wait_ge(s_ss, NT)
            dve.tensor_scalar(ss[:, 0:NT], ss[:, 0:NT], 1.0 / D, EPS, ALU.mult, ALU.add).then_inc(s_ms, 1)
            dve.wait_ge(s_std, 1)
            done(dve, dve.reciprocal(rstd[:, 0:NT], rstd[:, 0:NT]), s_dv)
            for i in range(NT):
                dve.tensor_scalar(xn[:, i, :], x_sb[:, i, :], rstd[:, i:i + 1], None, ALU.mult).then_inc(s_xn, 1)

            def mod_half(n):
                acc = mod_acc[:, n % 2, :]
                w = ring_a[:, 4 * (n % 2):4 * (n % 2) + 4, :].rearrange("p a b -> p (a b)")\
                    .rearrange("p (k c) -> p k c", k=KD)
                if n >= 2:
                    half_used(dve, n - 2)
                dve.wait_ge(s_ada[n % 2], 32 * (n // 2 + 1))
                done(dve, dve.tensor_scalar(acc, w[:, 0, :], c_silu[:, 0:1], None, ALU.mult), s_dv)
                for k in range(1, KD):
                    ins = dve.scalar_tensor_tensor(out=acc, in0=w[:, k, :], scalar=c_silu[:, k:k + 1], in1=acc,
                                                   op0=ALU.mult, op1=ALU.add)
                    if k < KD - 1:
                        done(dve, ins, s_dv)
                    else:
                        ins.then_inc(s_accd, 1)

            def mod_row(n):
                ps = taken(dve, ("row", n))
                dst = {2: g1_row, 4: a2_row, 3: sh2_row, 5: g2_row}[ADA_HALVES[n][0]]
                at = slice(512 * ADA_HALVES[n][1], 512 * ADA_HALVES[n][1] + 512)
                if ADA_HALVES[n][0] == 4:
                    ins = dve.scalar_tensor_tensor(out=dst[:, at], in0=ps[:, :], scalar=1.0, in1=dst[:, at],
                                                   op0=ALU.add, op1=ALU.mult)
                else:
                    ins = dve.tensor_copy(dst[:, at], ps[:, :])
                ins.then_inc(freeing(("row", n)), 1)

            for n in range(4):
                mod_half(n)
            cols = taken(dve, "mod_cols")
            dve.wait_ge(s_n1, 16)
            done(dve, dve.scalar_tensor_tensor(out=a1_col[:, :], in0=cols[:, 0:8], scalar=1.0, in1=n1_col[:, :],
                                               op0=ALU.add, op1=ALU.mult), s_dv)
            dve.tensor_copy(sh1_col[:, :], cols[:, 8:16]).then_inc(freeing("mod_cols"), 1)
            mod_half(4)
            for n in range(5, 12):
                mod_half(n)
                mod_row(n - 1)
            mod_row(11)
            emptied(dve, ("row", 11))
            for n in range(V_COLS // 256):
                for i in range(NT):
                    ps = taken(dve, ("v", n, i))
                    dve.tensor_copy(v_sb[:, i, 256 * n:256 * n + 256], ps[:, 0:256]).then_inc(freeing(("v", n, i)), 1)

            dve.wait_ge(s_const, 7)

            def soft_in(J):
                i, j = JOBS[J]
                kind, maps, scale, slope, _, c = plan[j]
                n = len(key_tiles(i, j)) * P
                nd = ndist_w[:, 2 * P - n:2 * P] if kind == "C" else ndist[:, S - n:S]
                for m in range(first_map[J], first_map[J] + len(maps)):
                    ps = taken(dve, ("s", m))
                    map_bufs_free(dve, m)
                    dve.scalar_tensor_tensor(out=Sb[:, m % 4, 0:n], in0=nd, scalar=slope / scale, in1=ps[:, 0:n],
                                             op0=ALU.mult, op1=ALU.add).then_inc(freeing(("s", m)), 1)
                    emptied(dve, ("s", m))
                    done(dve, dve.tensor_reduce(mx[:, m:m + 1], Sb[:, m % 4, 0:n], AX, ALU.max), s_dv)
                    if kind == "C":
                        dve.tensor_scalar(nmax[:, m:m + 1], mx[:, m:m + 1], -scale, nsinks[:, c:c + 1],
                                          ALU.mult, ALU.min).then_inc(s_nm, 1)
                    else:
                        dve.tensor_scalar(nmax[:, m:m + 1], mx[:, m:m + 1], -scale, None, ALU.mult).then_inc(s_nm, 1)

            def post(J):
                i, j = JOBS[J]
                kind, maps, _, _, _, c = plan[j]
                m = first_map[J]
                dve.wait_ge(s_exp, m + len(maps))
                if kind == "A":
                    r = ra[:, i * NA + j, :]
                    done(dve, dve.reciprocal(r, den[:, m:m + 2]), s_dv)
                    done(dve, dve.tensor_tensor(r[:, 1:2], r[:, 1:2], lam_s[:, 5:6], ALU.mult), s_dv)
                    n = len(key_tiles(i, j)) * P
                    one, two = Sb[:, m % 4, 0:n], Sb[:, (m + 1) % 4, 0:n]
                    done(dve, dve.tensor_scalar(one, one, r[:, 0:1], None, ALU.mult), s_dv)
                    dve.scalar_tensor_tensor(out=one, in0=two, scalar=r[:, 1:2], in1=one,
                                             op0=ALU.mult, op1=ALU.add).then_inc(s_comb, 1)
                    return
                if kind == "C":
                    a = i * NCH + c
                    dve.wait_ge(s_es, a + 1)
                    done(dve, dve.tensor_tensor(den[:, m:m + 1], den[:, m:m + 1], esink[:, a:a + 1], ALU.add), s_dv)
                done(dve, dve.reciprocal(rden[:, i, j:j + 1], den[:, m:m + 1]), s_dv)

            def heads_out(i):
                taken(dve, ("o", i, 0))
                taken(dve, ("o", i, 1))
                if i:
                    taken(dve, ("oT", i - 1, 1))
                nA = NA * HD
                oa = o_sb[:, 0:nA]
                done(dve, dve.tensor_copy(oa, bank["O0"][:, 0:nA]), s_dv)
                done(dve, dve.tensor_tensor(rep[:, 0:nA], oa, oa, ALU.mult), s_dv)
                done(dve, dve.tensor_reduce(sso[:, i, :, 0], rep[:, 0:nA].rearrange("p (h d) -> p h d", d=HD),
                                            AX, ALU.add), s_dv)
                dve.tensor_scalar(sso[:, i, :, 0], sso[:, i, :, 0], 1.0 / HD, EPS, ALU.mult, ALU.add).then_inc(s_sso, 1)
                for b, lo, hi in (("O0", NA, 8), ("O1", 8, NHEADS)):
                    dve.tensor_tensor(o_sb[:, lo * HD:hi * HD].rearrange("p (h d) -> p h d", d=HD),
                                      bank[b][:, (lo % 8) * HD:512].rearrange("p (h d) -> p h d", d=HD),
                                      rden[:, i, lo:hi].unsqueeze(2).to_broadcast([P, hi - lo, HD]),
                                      ALU.mult).then_inc(free[b], 1)
                dve.wait_ge(s_so, i + 1)
                done(dve, dve.reciprocal(sso[:, i, :, 1], sso[:, i, :, 1]), s_dv)
                o4 = oa.rearrange("p (h d) -> p h d", d=HD)
                done(dve, dve.tensor_tensor(o4, o4, sso[:, i, :, 1].unsqueeze(2).to_broadcast([P, NA, HD]),
                                            ALU.mult), s_dv)
                dve.tensor_tensor(o4, o4, subln[:, :].unsqueeze(1).to_broadcast([P, NA, HD]), ALU.mult).then_inc(s_o, 1)

            def add_mixer(i):
                for half in range(2):
                    at = slice(512 * half, 512 * half + 512)
                    ps = taken(dve, ("y", i, half))
                    dve.tensor_tensor(mod_acc[:, half, :], ps[:, :], g1_row[:, at], ALU.mult)\
                       .then_inc(freeing(("y", i, half)), 1)
                    emptied(dve, ("y", i, half))
                    ins = dve.tensor_tensor(x_sb[:, i, at], x_sb[:, i, at], mod_acc[:, half, :], ALU.add)
                    done(dve, ins, s_x1 if half else s_dv)

            for J in range(N + 6):
                if J < N:
                    soft_in(J)
                if 1 <= J <= N:
                    post(J - 1)
                if J >= 2 and (J - 2) % NHEADS == NHEADS - 1:
                    heads_out((J - 2) // NHEADS)
                if J >= 6 and (J - 6) % NHEADS == NHEADS - 1:
                    add_mixer((J - 6) // NHEADS)

            flat = mod_acc[:, :, :].rearrange("p a b -> p (a b)")
            for i in range(NT):
                done(dve, dve.tensor_tensor_reduce(out=flat, in0=x_sb[:, i, :], in1=x_sb[:, i, :], scale=1.0,
                                                   scalar=0.0, op0=ALU.mult, op1=ALU.add,
                                                   accum_out=ss[:, NT + i:NT + i + 1]), s_dv)
            dve.tensor_scalar(ss[:, NT:2 * NT], ss[:, NT:2 * NT], 1.0 / D, EPS, ALU.mult, ALU.add).then_inc(s_ms, 1)
            dve.wait_ge(s_std, 2)
            done(dve, dve.reciprocal(rstd[:, NT:2 * NT], rstd[:, NT:2 * NT]), s_dv)
            for i in range(NT):
                done(dve, dve.scalar_tensor_tensor(out=h2[:, i, :], in0=x_sb[:, i, :], scalar=rstd[:, NT + i:NT + i + 1],
                                                   in1=a2_row[:, :], op0=ALU.mult, op1=ALU.mult), s_dv)
                dve.tensor_tensor(h2[:, i, :], h2[:, i, :], sh2_row[:, :], ALU.add).then_inc(s_h2, 1)
            dve.wait_ge(s_h2, NT)

            def best16(src, values, places, copy):
                step = s_dv
                for a, v in zip(src, values):
                    last = dve.max(v[:, 0:8], a)
                    if a is not src[-1]:
                        last.then_inc(step, 1)
                        tally[step.name] += 1
                done(dve, last, step)
                for a, v, q, t in zip(src, values, places, copy):
                    dve.max_index(q[:, 0:8], v[:, 0:8], a)
                    last = dve.match_replace(t, v[:, 0:8], a, -3.0e38)
                    if a is not src[-1]:
                        last.then_inc(step, 1)
                        tally[step.name] += 1
                done(dve, last, step)
                for t, v in zip(copy, values):
                    last = dve.max(v[:, 8:16], t)
                    if t is not copy[-1]:
                        last.then_inc(step, 1)
                        tally[step.name] += 1
                done(dve, last, step)
                for t, v, q in zip(copy, values, places):
                    last = dve.max_index(q[:, 8:16], v[:, 8:16], t)
                    if t is not copy[-1]:
                        last.then_inc(step, 1)
                        tally[step.name] += 1
                done(dve, last, step)

            for g in range(4):
                for i in range(NT):
                    n = g * NT + i
                    emptied(dve, ("sc", g, i))
                    heads = [(2 * g + a, s) for a in range(2) for s in range(2)]
                    best16([sc[:, n % 8, P * q:P * q + P] for q in range(4)],
                           [sv[:, i, h, s, :] for h, s in heads], [si[:, i, h, s, :] for h, s in heads],
                           [rep[:, P * q:P * q + P] for q in range(4)])
                    for a in range(2):
                        h = 2 * g + a
                        ins = dve.tensor_tensor(cand[:, a, :, :],
                                                sv[:, i, h, 0, :].unsqueeze(2).to_broadcast([P, TOPK, TOPK]),
                                                sv[:, i, h, 1, :].unsqueeze(1).to_broadcast([P, TOPK, TOPK]), ALU.add)
                        if a:
                            ins.then_inc(s_scu, 1)
                    dve.wait_ge(s_scu, n + 1)
                    best16([cand[:, a, :, :].rearrange("p a b -> p (a b)") for a in range(2)],
                           [topv[:, i, 2 * g + a, :] for a in range(2)], [topp[:, i, 2 * g + a, :] for a in range(2)],
                           [rep[:, 256 * a:256 * a + 256] for a in range(2)])

            HK = PH * TOPK
            for i in range(NT):
                pos = topp[:, i, :, :].rearrange("p h k -> p (h k)")
                done(dve, dve.tensor_scalar(side_u[:, 0, :], pos, 4, None, ALU.logical_shift_right), s_dv)
                done(dve, dve.tensor_scalar(side_u[:, 1, :], pos, 15, None, ALU.bitwise_and), s_dv)
                done(dve, dve.tensor_copy(side_f[:, :, :], side_u[:, :, :]), s_dv)
                done(dve, dve.tensor_copy(sif[:, :, :, :], si[:, i, :, :, :]), s_dv)
                for s in range(2):
                    hot = onehot.rearrange("p (a b) -> p a b", b=TOPK)
                    done(dve, dve.tensor_tensor(hot, iota16[:, :].unsqueeze(1).to_broadcast([P, HK, TOPK]),
                                                side_f[:, s, :].unsqueeze(2).to_broadcast([P, HK, TOPK]),
                                                ALU.is_equal), s_dv)
                    for h in range(PH):
                        hot = onehot.rearrange("p (h k a) -> p h k a", k=TOPK, a=TOPK)[:, h, :, :]
                        ins = dve.tensor_tensor(hot, hot, sif[:, h, s, :].unsqueeze(1).to_broadcast([P, TOPK, TOPK]),
                                                ALU.mult)
                        tally[s_dv.name] += 1
                        ins.then_inc(s_dv, 1)
                    dve.wait_ge(s_dv, tally[s_dv.name])
                    done(dve, dve.tensor_reduce(key_f[:, s, :], onehot.rearrange("p (a b) -> p a b", b=TOPK),
                                                AX, ALU.add), s_dv)
                done(dve, dve.scalar_tensor_tensor(out=eidx[:, i, :], in0=key_f[:, 0, :], scalar=float(NKEYS),
                                                   in1=key_f[:, 1, :], op0=ALU.mult, op1=ALU.add), s_dv)
                gt = gate[:, i, :].rearrange("p (h k) -> p h k", k=TOPK)
                dve.tensor_tensor(gt, topv[:, i, :, :], topv[:, i, :, 0:1].to_broadcast([P, PH, TOPK]),
                                  ALU.subtract).then_inc(s_gd, 1)
                dve.wait_ge(s_ge, i + 1)
                done(dve, dve.tensor_reduce(gsum[:, :], gt, AX, ALU.add), s_dv)
                done(dve, dve.reciprocal(gsum[:, :], gsum[:, :]), s_dv)
                done(dve, dve.tensor_tensor(gt, gt, gsum[:, :].unsqueeze(2).to_broadcast([P, PH, TOPK]),
                                            ALU.mult), s_dv)
                if i == NT - 1:
                    for half in range(2):
                        dve.memset(y[:, 2 * half:2 * half + 2, :], 0.0).then_inc(s_used, 1)
                    dve.wait_ge(s_used, 2)
                done(dve, dve.tensor_copy(key_f[:, 0, 0:1], key_f[:, 0, 0:1]), s_idx)

            def head(i, h):
                G = h + i * PH
                for j in range(TOPK):
                    dve.wait_ge(s_got[j], 16 * (2 * G + 1))
                    dve.wait_ge(s_used, 2 + 32 * G + j)
                    dve.scalar_tensor_tensor(out=junk[:, :], in0=ring[j], scalar=1.0, in1=h2[:, i, :], op0=ALU.mult,
                                             op1=ALU.mult, accum_out=dots[:, j:j + 1]).then_inc(s_used, 1)
                dve.wait_ge(s_gel, G + 1)
                dve.tensor_tensor(wgt[:, :], act_g[:, :], gate[:, i, bass.ds(h * TOPK, TOPK)], ALU.mult).then_inc(s_w, 1)
                dve.wait_ge(s_w, G + 1)
                for j in range(TOPK):
                    dve.wait_ge(s_got[j], 16 * (2 * G + 2))
                    dve.wait_ge(s_used, 2 + 32 * G + TOPK + j)
                    dve.scalar_tensor_tensor(out=y[:, i, :], in0=ring[j], scalar=wgt[:, j:j + 1], in1=y[:, i, :],
                                             op0=ALU.mult, op1=ALU.add).then_inc(s_used, 1)

            for i in range(NT):
                with dve.Fori(0, PH) as h:
                    head(i, h)
                dve.wait_ge(s_used, 2 + 32 * PH * (i + 1))
                if i == 0:
                    dve.wait_ge(s_fin, 16)
                done(dve, dve.tensor_tensor(y[:, i, :], y[:, i, :], g2_row[:, :], ALU.mult), s_dv)
                done(dve, dve.tensor_tensor(x_sb[:, i, :], x_sb[:, i, :], y[:, i, :], ALU.add), s_dv)
                q = slice(2 * NT + i, 2 * NT + i + 1)
                done(dve, dve.tensor_tensor_reduce(out=flat, in0=x_sb[:, i, :], in1=x_sb[:, i, :], scale=1.0,
                                                   scalar=0.0, op0=ALU.mult, op1=ALU.add, accum_out=ss[:, q]), s_dv)
                dve.tensor_scalar(ss[:, q], ss[:, q], 1.0 / D, EPS, ALU.mult, ALU.add).then_inc(s_f2, 1)
                dve.wait_ge(s_fs, i + 1)
                done(dve, dve.reciprocal(rstd[:, q], rstd[:, q]), s_dv)
                dve.scalar_tensor_tensor(out=x_sb[:, i, :], in0=x_sb[:, i, :], scalar=rstd[:, q], in1=g1_row[:, :],
                                         op0=ALU.mult, op1=ALU.mult).then_inc(s_res, 1)


def kernel(**inputs):
    import concourse.bacc as bacc
    from concourse.bass_utils import run_bass_kernel_spmd as run

    a = {n: np.asarray(v) for n, v in inputs.items()}
    qa, ka, va, qb, kb, vb, qc, kc, vc = np.split(
        np.arange(a["w_in"].shape[2]), np.cumsum([256, 256, 256, 384, 384, 384, 384, 128]))
    qc = qc.reshape(2, CG, HD).transpose(1, 0, 2).reshape(-1)
    order = np.concatenate([qa, ka, qb, kb, qc, kc, va, vb, vc])
    w_in = a["w_in"][0][:, order].reshape(KD, P, IN_TILES, P).transpose(2, 1, 0, 3).reshape(IN_TILES, P, D)
    wq = a["peer_wq"][0].reshape(KD, P, 2 * PH, P).transpose(2, 1, 0, 3).reshape(2 * PH, P, D)
    data = {
        "x": a["x"], "c_col": a["c"].reshape(KD, P).T, "norm1_col": a["norm1_g"].reshape(KD, P).T,
        "w_ada": a["w_ada"][0], "b_ada": a["b_ada"], "w_in": w_in, "w_out": a["w_out"][0],
        "lam_vecs": np.concatenate([a[n][0] for n in ("lam_q1", "lam_k1", "lam_q2", "lam_k2")]),
        "subln_row": a["subln_g"][0], "sinks_row": a["sinks"][0], "norm2_row": a["norm2_g"][0], "wq": wq,
        "keys_t": a["peer_keys"][0].transpose(3, 0, 1, 2).reshape(P, 2 * PH, NKEYS),
        "peer_u": a["peer_u"][0], "peer_v": a["peer_v"][0], "final_row": a["final_g"],
    }
    nc = bacc.Bacc("TRN2", target_bir_lowering=False, num_devices=1)
    arrays, args = {}, []
    for name, v in data.items():
        v = np.ascontiguousarray(v)
        arrays["in_" + name] = v
        args.append(nc.dram_tensor("in_" + name, v.shape, mybir.dt.from_np(v.dtype), kind="ExternalInput").ap())
    args.append(nc.dram_tensor("out_0", (1, S, D), mybir.dt.float32, kind="ExternalOutput").ap())
    peer_block_kernel(nc, *args)
    return run(nc, [arrays], core_ids=[0]).results[0]["out_0"]
```

```python
import numpy as np
import concourse.bass as bass
from concourse import mybir
from contextlib import ExitStack

P = 128
D, S = 1024, 512
KD = D // P
NT = S // P
HD = 64
NA, NB, NCH = 4, 6, 6
CG = NCH // 2
NHEADS = NA + NB + NCH
QK_TILES, V_COLS = 14, 768
IN_TILES = QK_TILES + V_COLS // P
PH, TOPK, NKEYS = 8, 16, 128
NCHUNK = NKEYS
GT = 1
DT = S - GT * P
GB = 32
AHEAD = 8
EPS = 1e-6
LAM_INIT = 0.8 - 0.6
MASKED = -1e30
SLOPES = [2.0 ** (-8.0 * n / NHEADS) for n in range(1, NHEADS + 1)]


def head_plan():
    plan = []
    for h in range(NA):
        maps = [(h // 2, 2 + h // 2, 64 * (h % 2) + 32 * m, 32) for m in range(2)]
        plan.append(("A", maps, 32 ** -0.5, SLOPES[NCH + h], h * HD, None))
    for h in range(NB):
        plan.append(("B", [(4 + h // 2, 7 + h // 2, 64 * (h % 2), 64)], 64 ** -0.5,
                     SLOPES[NCH + NA + h], 256 + h * HD, None))
    for h in range(NCH):
        kv = h // CG
        plan.append(("C", [(10 + h % CG, 13, 64 * kv, 64)], 64 ** -0.5, SLOPES[h], 640 + kv * HD, h))
    return plan


def peer_block_kernel(nc, x, c_col, norm1_col, w_ada, b_ada, w_in, w_out, lam_vecs, subln_row, sinks_row,
                      norm2_row, wq, keys_t, peer_u, peer_v, u_t, final_row, out):
    f32, u32, f32r = mybir.dt.float32, mybir.dt.uint32, mybir.dt.float32r
    ALU, ACT, AX = mybir.AluOpType, mybir.ActivationFunctionType, mybir.AxisListType.X
    ctx = ExitStack()
    with ctx:
        def sb(name, shape, dt=f32):
            return ctx.enter_context(nc.sbuf_tensor(name, shape, dt))

        def sem(name):
            return ctx.enter_context(nc.semaphore(name))

        base = -(-nc.sbuf_base // 32) * 32
        slab = sb("slab", [P, 184 * 256])

        def at(name, kib, shape, dt=f32):
            return nc.alloc_sbuf_tensor_at(name, shape, dt, offset=base + int(kib * 1024))

        x_sb = at("x_sb", 0, [P, NT, D])
        h2 = at("h2", 16, [P, NT, D])
        hT = at("hT", 32, [P, KD, S])
        ring_w = at("ring_w", 48, [P, 8, D])
        ring_a = at("ring_a", 80, [P, 8, D])
        qkT = at("qkT", 112, [P, QK_TILES, S])
        keys = at("keys", 140, [P, 2 * PH, NKEYS])
        a2_row = at("a2_row", 148, [P, D])
        sh2_row = at("sh2_row", 152, [P, D])
        v_sb = at("v_sb", 156, [P, NT, V_COLS])
        g1_row = at("g1_row", 168, [P, D])
        g2_row = at("g2_row", 172, [P, D])
        mod_acc = at("mod_acc", 176, [P, 2, 512])
        o_sb = at("o_sb", 180, [P, D])
        a_act = at("a_act", 20, [P, AHEAD, DT])
        y0 = at("y0", 32, [P, D])
        g_in = at("g_in", 36, [P, 2, DT // GB, 4, GB])
        cols = at("cols", 36, [P, 3, DT])
        v_raw = at("v_raw", 48, [P, 2, D])
        h_hi = at("h_hi", 56, [P, KD, DT], f32r)
        h_lo = at("h_lo", 68, [P, KD, DT], f32r)
        u_raw = at("u_raw", 80, [P, 2, D])
        u_hi = at("u_hi", 88, [P, 2, D], f32r)
        u_lo = at("u_lo", 96, [P, 2, D], f32r)
        v_hi = at("v_hi", 112, [P, 2, D], f32r)
        v_lo = at("v_lo", 120, [P, 2, D], f32r)
        g_out = [at("g_out0", 112, [P, P, GB]), at("g_out1", 140, [P, P, GB])]
        hot_j = at("hot_j", 128, [P, 2, 4, P])
        hot_i = at("hot_i", 132, [P, 2, 4, P])
        w_f = at("w_f", 128, [P, DT])
        w_hi = at("w_hi", 130, [P, 2, DT], f32r)
        w_lo = at("w_lo", 133, [P, 2, DT], f32r)
        rows = [at(f"row{j}", k, [P, D]) for j, k in enumerate((104, 108, 140, 144, 148, 152, 156, 160))]
        ident = sb("ident", [P, P])
        ones = sb("ones", [P, P])
        ndist = sb("ndist", [P, S])
        ndist_w = sb("ndist_w", [P, 2 * P])
        b_half = sb("b_half", [1, 2, 512])
        c_in = sb("c_in", [P, KD])
        c_silu = sb("c_silu", [P, KD])
        c_tmp = sb("c_tmp", [P, KD])
        n1_col = sb("n1_col", [P, KD])
        a1_col = sb("a1_col", [P, KD])
        sh1_col = sb("sh1_col", [P, KD])
        lam_in = sb("lam_in", [P, 4, 32])
        lam_prod = sb("lam_prod", [P, 2, 32])
        lam_s = sb("lam_s", [P, 8])
        subln = sb("subln", [P, HD])
        sinks = sb("sinks", [P, NCH])
        nsinks = sb("nsinks", [P, NCH])
        ss = sb("ss", [P, 3 * NT])
        rstd = sb("rstd", [P, 3 * NT])
        MAPS = NA + NHEADS
        mx = sb("mx", [P, NT * MAPS])
        nmax = sb("nmax", [P, NT * MAPS])
        den = sb("den", [P, NT * MAPS])
        esink = sb("esink", [P, NT * NCH])
        rden = sb("rden", [P, NT, NHEADS])
        ra = sb("ra", [P, NT * NA, 2])
        sso = sb("sso", [P, NT, NA, 2])
        si = sb("si", [P, NT, PH, 2, TOPK], u32)
        topp = sb("topp", [P, NT, PH, TOPK], u32)
        rep = mod_acc[:, 0, :]
        cand = mod_acc[:, 1, :].rearrange("p (h a b) -> p h a b", a=TOPK, b=TOPK)
        side_u = sb("side_u", [P, 2, PH * TOPK], u32)
        eidx = sb("eidx", [P, PH * TOPK], u32)
        gate = sb("gate", [P, NT, PH * TOPK])
        gsum = sb("gsum", [P, PH])
        iota16 = sb("iota16", [P, TOPK])
        iota_k = sb("iota_k", [P, NKEYS])
        stage = sb("stage", [P, 4], u32)
        four = sb("four", [P, 2, 4])
        dots = sb("dots", [P, 2])
        act_g = sb("act_g", [P, 2])
        wgt = sb("wgt", [P, 2])
        late = v_sb[:, :, :].rearrange("p t c -> p (t c)")
        sv = late[:, 0:1024].rearrange("p (t h s k) -> p t h s k", t=NT, h=PH, s=2)
        topv = late[:, 1024:1536].rearrange("p (t h k) -> p t h k", t=NT, h=PH)
        sif = late[:, 1536:1792].rearrange("p (h s k) -> p h s k", h=PH, s=2)
        side_f = late[:, 1792:2048].rearrange("p (s k) -> p s k", s=2)
        key_f = late[:, 2048:3072].rearrange("p (t s k) -> p t s k", t=NT, s=2)
        xn = qkT[:, 0:8, :].rearrange("p (t a) s -> p t (a s)", t=NT)
        Sb = hT[:, 0:4, :]
        pT = hT[:, 4:6, :]
        oT = hT[:, 6, :].rearrange("p (a b) -> p a b", b=P), hT[:, 7, :].rearrange("p (a b) -> p a b", b=P)
        junk = o_sb
        w_outs = ring_w
        onehot = ring_w[:, 0:2, :].rearrange("p a b -> p (a b)")
        sc = qkT[:, 0:8, :]
        qT = qkT[:, 8:11, :]

        bank = {n: ctx.enter_context(nc.psum_tensor("bank_" + n, [P, 512], f32))
                for n in ("S0", "S1", "S2", "T0", "T1", "O0", "O1", "G")}
        full = {n: sem("full_" + n) for n in bank}
        free = {n: sem("free_" + n) for n in bank}
        turn = {}
        fillings = dict.fromkeys(bank, 0)

        s_x, s_out = sem("x_loaded"), sem("out_stored")
        s_c, s_n1, s_lam, s_small = sem("c_loaded"), sem("norm1_loaded"), sem("lam_loaded"), sem("rows_loaded")
        s_ada = [sem("ada_loaded0"), sem("ada_loaded1")]
        s_win = [sem(f"w_loaded{j}") for j in range(8)]
        s_wout, s_keys, s_fin = sem("w_out_loaded"), sem("keys_loaded"), sem("final_loaded")
        s_wq = [sem(f"wq_loaded{j}") for j in range(8)]
        s_const = sem("constants_made")
        s_accd, s_modu, s_rows = sem("mod_summed"), sem("mod_used"), sem("mod_rows_ready")
        s_winu, s_wqu = sem("w_in_used"), sem("wq_used")
        s_dv, s_ac = sem("vector_steps"), sem("scalar_steps")
        s_ce, s_ss, s_ms, s_std, s_xn = sem("exp_c"), sem("squares"), sem("mean_squares"), sem("std"), sem("xn_ready")
        s_a1, s_hT, s_qk, s_v = sem("mod_cols_ready"), sem("hT_ready"), sem("qk_ready"), sem("v_ready")
        s_lp, s_le = sem("lam_sums"), sem("lam_exps")
        s_nm, s_exp, s_es, s_comb = sem("nmax_ready"), sem("exp_done"), sem("sink_exp"), sem("probs_ready")
        s_pt, s_pTr, s_pv = sem("probs_transposed"), sem("pT_ready"), sem("pv_done")
        s_sso, s_so, s_o, s_oTr, s_y = sem("o_squares"), sem("o_std"), sem("o_ready"), sem("oT_ready"), sem("oproj_done")
        s_x1, s_h2, s_h2T = sem("x1_ready"), sem("h2_ready"), sem("h2T_ready")
        s_qT, s_qTu, s_sc, s_scu = sem("qT_ready"), sem("qT_used"), sem("scores_ready"), sem("scores_used")
        s_gd, s_ge, s_idx = sem("gate_shifted"), sem("gate_exp"), sem("experts_ready")
        s_got = [sem(f"row_got{j}") for j in range(8)]
        s_stg, s_clear = sem("staged"), sem("slots_cleared")
        s_dot, s_dgelu, s_wgt, s_acc = sem("row_dots"), sem("row_gelus"), sem("row_weights"), sem("row_sums")
        s_hhi, s_hlo = sem("h_hi_ready"), sem("h_lo_ready")
        s_u, s_v = [sem("u_loaded0"), sem("u_loaded1")], [sem("v_loaded0"), sem("v_loaded1")]
        s_uhi, s_ulo, s_vhi, s_vlo = sem("u_hi_ready"), sem("u_lo_ready"), sem("v_hi_ready"), sem("v_lo_ready")
        s_a, s_gelu, s_pw, s_whi, s_w = sem("a_done"), sem("gelu_done"), sem("w_product"), sem("w_hi"), sem("w_ready")
        s_yv = sem("v_product_done")
        s_g = [sem("gates_loaded0"), sem("gates_loaded1")]
        s_four = sem("four_ready")
        s_j, s_i, s_gm, s_gt = sem("hot_j_ready"), sem("hot_i_ready"), sem("gates_made"), sem("gates_taken")
        s_gst = [sem("gates_stored0"), sem("gates_stored1")]
        s_x2, s_f2, s_fs, s_res = sem("x2_ready"), sem("x2_squares"), sem("x2_std"), sem("result_ready")

        gates = nc.dram_tensor("gates", [DT // GB, P, NCHUNK, GB], f32).ap()
        y_bank = [[bank["S0"], bank["S1"]], [bank["S2"], bank["T0"]], [bank["T1"], bank["G"]]]

        def after(eng, s, n):
            if isinstance(n, int) and n < 1:
                return
            eng.wait_ge(s, n)

        def within(i, last=NCHUNK - 1):
            return not isinstance(i, int) or i <= last

        def chunk_loop(eng, body, looped=(1, 14)):
            turns = NCHUNK // AHEAD
            for t in range(looped[0]):
                for c in range(AHEAD):
                    body(t * AHEAD + c, c)
            with eng.Fori(*looped) as t:
                for c in range(AHEAD):
                    body(t * AHEAD + c, c)
            for t in range(looped[1], turns):
                for c in range(AHEAD):
                    body(t * AHEAD + c, c)

        def over(i, c, n):
            return i // n if isinstance(i, int) else (i - c) // n + c // n

        def gate_blocks(eng, tile, body):
            if tile == 0:
                for b in range(4):
                    body(b, b % 2)
            else:
                with eng.Fori(2 * tile, 2 * tile + 2) as two:
                    for b in range(2):
                        body(2 * two + b, b)

        tally = {}

        def done(eng, ins, s):
            tally[s.name] = tally.get(s.name, 0) + 1
            ins.then_inc(s, 1)
            eng.wait_ge(s, tally[s.name])

        plan = head_plan()
        JOBS = [(i, j) for i in range(NT) for j in range(NHEADS)]
        first_map = []
        for i, j in JOBS:
            first_map.append(i * MAPS + sum(len(plan[a][1]) for a in range(j)))
        ADA_ORDER = [1, 0, 2, 4, 3, 5]
        ADA_HALVES = [(s, b) for s in ADA_ORDER for b in range(2)]

        N = len(JOBS)

        def key_tiles(i, j):
            return range(max(0, i - 1), i + 1) if plan[j][0] == "C" else range(i + 1)

        block = ctx.enter_context(nc.Block())

        @block.tensor
        def _(pe):
            def take(b, key):
                if fillings[b]:
                    pe.wait_ge(free[b], fillings[b])
                fillings[b] += 1
                turn[key] = (b, fillings[b])
                return bank[b]

            def emptied(key):
                b, n = turn[key]
                pe.wait_ge(free[b], n)

            pe.wait_ge(s_const, 6)
            mcols = take("G", "mod_cols")
            for n in range(4):
                pe.wait_ge(s_accd, n + 1)
                for m in range(4):
                    at = n * 4 + m
                    pe.matmul(mcols[:, at:at + 1], mod_acc[:, n % 2, m * P:m * P + P], ones[:, 0:1],
                              start=True, stop=False)
                    mm = pe.matmul(mcols[:, at:at + 1], b_half[0:1, n % 2, m * P:m * P + P], ones[0:1, 0:1],
                                   start=False, stop=True)
                mm.then_inc(full["G"] if n == 3 else s_modu, 1)
            for k in range(KD):
                b = f"T{k % 2}"
                ps = take(b, ("xT", k))
                for i in range(NT):
                    if k == 0:
                        pe.wait_ge(s_xn, i + 1)
                    mm = pe.transpose(ps[:, i * P:i * P + P], xn[:, i, k * P:k * P + P], ident[:, :])
                mm.then_inc(full[b], 1)

            def mod_row(n):
                ps = take("G", ("row", n))
                pe.wait_ge(s_accd, n + 1)
                pe.matmul(ps[:, :], ones[:, :], mod_acc[:, n % 2, :], start=True, stop=False)
                pe.matmul(ps[:, :], ones[0:1, :], b_half[0:1, n % 2, :], start=False, stop=True)\
                    .then_inc(full["G"], 1)

            for e in range(QK_TILES):
                b = f"S{e % 3}"
                ps = take(b, ("qk", e))
                pe.wait_ge(s_win[e % 8], 16 * (e // 8 + 1))
                for k in range(KD):
                    if e == 0:
                        emptied(("xT", k))
                    mm = pe.matmul(ps[:, :], ring_w[:, e % 8, k * P:k * P + P], hT[:, k, :],
                                   start=(k == 0), stop=(k == KD - 1))
                mm.then_inc(full[b], 1)
                if 2 <= e < 10:
                    mod_row(e + 2)
            for n in range(V_COLS // 256):
                e = QK_TILES + 2 * n
                for a in (e, e + 1):
                    pe.wait_ge(s_win[a % 8], 16 * (a // 8 + 1))
                w = ring_w[:, e % 8:e % 8 + 2, :].rearrange("p a (k c) -> p a k c", k=KD)
                for i in range(NT):
                    b = f"O{i % 2}"
                    ps = take(b, ("v", n, i))
                    for k in range(KD):
                        mm = pe.matmul(ps[:, 0:256], hT[:, k, i * P:i * P + P], w[:, :, k, :],
                                       start=(k == 0), stop=(k == KD - 1))
                    mm.then_inc(full[b], 1)

            for e in range(QK_TILES - 3, QK_TILES):
                emptied(("qk", e))
            maps_done = [0]

            def scores(J):
                i, j = JOBS[J]
                kt = key_tiles(i, j)
                for m, (qt, kk, part, rows) in enumerate(plan[j][1]):
                    b = f"S{maps_done[0] % 3}"
                    maps_done[0] += 1
                    ps = take(b, ("s", first_map[J] + m))
                    pe.matmul(ps[:, 0:len(kt) * P], qkT[part:part + rows, qt, i * P:i * P + P],
                              qkT[part:part + rows, kk, kt[0] * P:(kt[-1] + 1) * P],
                              start=True, stop=True).then_inc(full[b], 1)

            def transpose_probs(J):
                i, j = JOBS[J]
                b = f"T{J % 2}"
                ps = take(b, ("pT", J))
                if plan[j][0] == "A":
                    pe.wait_ge(s_comb, i * NA + j + 1)
                else:
                    pe.wait_ge(s_exp, first_map[J] + 1)
                for n, kt in enumerate(key_tiles(i, j)):
                    mm = pe.transpose(ps[:, n * P:n * P + P], Sb[:, first_map[J] % 4, n * P:n * P + P], ident[:, :])
                mm.then_inc(full[b], 1)

            def pv(J):
                i, j = JOBS[J]
                b = f"O{j // 8}"
                ps = take(b, ("o", i, j // 8)) if j % 8 == 0 else bank[b]
                if J == 0:
                    emptied(("v", 2, 2))
                    emptied(("v", 2, 3))
                emptied(("pT", J))
                col = plan[j][4]
                kt = key_tiles(i, j)
                for n, t in enumerate(kt):
                    mm = pe.matmul(ps[:, (j % 8) * HD:(j % 8) * HD + HD], pT[:, J % 2, n * P:n * P + P],
                                   v_sb[:, t, col:col + HD], start=(n == 0), stop=(n == len(kt) - 1))
                mm.then_inc(full[b] if j % 8 == 7 else s_pv, 1)

            def out_proj(i):
                for half in range(2):
                    b = f"T{half}"
                    ps = take(b, ("oT", i, half))
                    pe.wait_ge(s_o, i + 1)
                    for n in range(4):
                        k = half * 4 + n
                        mm = pe.transpose(ps[:, n * P:n * P + P], o_sb[:, k * P:k * P + P], ident[:, :])
                    mm.then_inc(full[b], 1)
                if i == 0:
                    pe.wait_ge(s_wout, 16)
                emptied(("oT", i, 0))
                emptied(("oT", i, 1))
                for half, b in enumerate(("G", "T0")):
                    ps = take(b, ("y", i, half))
                    for k in range(KD):
                        mm = pe.matmul(ps[:, :], oT[k // 4][:, k % 4, :],
                                       w_outs[:, k, half * 512:half * 512 + 512],
                                       start=(k == 0), stop=(k == KD - 1))
                    mm.then_inc(full[b], 1)

            scores(0)
            for J in range(N + 5):
                if J + 1 < N:
                    scores(J + 1)
                if 1 <= J <= N:
                    transpose_probs(J - 1)
                if 2 <= J < N + 2:
                    pv(J - 2)
                if J >= 5 and (J - 5) % NHEADS == NHEADS - 1:
                    out_proj((J - 5) // NHEADS)

            pe.wait_ge(s_h2, NT)
            for k in range(KD):
                b = f"T{k % 2}"
                ps = take(b, ("h2T", k))
                for i in range(NT):
                    mm = pe.transpose(ps[:, i * P:i * P + P], h2[:, i, k * P:k * P + P], ident[:, :])
                mm.then_inc(full[b], 1)
            kb = ["T0", "T1", "O0", "O1"]

            def key_scores(e):
                emptied(("q", e))
                for i in range(NT):
                    ps = take(kb[i], ("sc", e // 4, i)) if e % 4 == 0 else bank[kb[i]]
                    mm = pe.matmul(ps[:, (e % 4) * P:(e % 4) * P + P], qT[:, e % 3, i * P:i * P + P], keys[:, e, :],
                                   start=True, stop=True)
                    if e % 4 == 3:
                        mm.then_inc(full[kb[i]], 1)
                if e % 4 != 3:
                    mm.then_inc(s_qTu, 1)

            for e in range(2 * PH):
                b = f"S{e % 3}"
                ps = take(b, ("q", e))
                pe.wait_ge(s_wq[e % 8], 16 * (e // 8 + 1))
                for k in range(KD):
                    if e == 0:
                        emptied(("h2T", k))
                    mm = pe.matmul(ps[:, :], ring_a[:, e % 8, k * P:k * P + P], hT[:, k, :],
                                   start=(k == 0), stop=(k == KD - 1))
                mm.then_inc(full[b], 1)
                if e == 0:
                    pe.wait_ge(s_keys, 16)
                if e >= 1:
                    key_scores(e - 1)
            key_scores(2 * PH - 1)

            def a_chunk(i, c):
                if not within(i):
                    return
                ps = bank[f"O{c % 2}"]
                after(pe, s_gelu, i - 1)
                pe.wait_ge(s_uhi, i + 1)
                pe.wait_ge(s_ulo, i + 1)
                q = c % 2
                for k in range(KD):
                    kk = slice(k * P, k * P + P)
                    pe.matmul(ps[:, 0:DT], u_hi[:, q, kk], h_hi[:, k, :], start=(k == 0), stop=False)
                    pe.matmul(ps[:, 0:DT], u_hi[:, q, kk], h_lo[:, k, :], start=False, stop=False)
                    mm = pe.matmul(ps[:, 0:DT], u_lo[:, q, kk], h_hi[:, k, :], start=False, stop=(k == KD - 1))
                mm.then_inc(s_a, 1)

            for i in range(NT):
                b, n = turn[("sc", 3, i)]
                pe.wait_ge(free[b], n)
            for k in range(KD):
                pe.wait_ge(s_hlo, k + 1)
                pe.wait_ge(s_hhi, k + 1)
            for i in range(AHEAD):
                a_chunk(i, i)

            for tile in range(NT - GT):
                ps = take("G", ("cols", tile))
                pe.wait_ge(s_idx, tile + 1)
                for n, m in enumerate((key_f[:, tile + GT, 0, :], key_f[:, tile + GT, 1, :], gate[:, tile + GT, :])):
                    mm = pe.transpose(ps[:, n * P:n * P + P], m, ident[:, :])
                mm.then_inc(full["G"], 1)

                def block_gates(tb, parity):
                    for b in range(GB // 4):
                        B = tb * (GB // 4) + b
                        ps = bank[f"T{b % 2}"]
                        after(pe, s_gt, B - 1)
                        pe.wait_ge(s_j, B + 1)
                        pe.wait_ge(s_i, B + 1)
                        for tok in range(4):
                            mm = pe.matmul(ps[:, tok * P:tok * P + P], hot_j[:, b % 2, tok, :], hot_i[:, b % 2, tok, :],
                                           start=True, stop=True)
                        mm.then_inc(s_gm, 1)

                gate_blocks(pe, tile, block_gates)
            emptied(("cols", NT - GT - 1))
            pe.wait_ge(s_gt, DT // 4)

            def v_chunk(i, c):
                pe.wait_ge(s_w, i + 1)
                pe.wait_ge(s_vlo, i + 1)
                q = c % 2
                first, last = isinstance(i, int) and i == 0, isinstance(i, int) and i == NCHUNK - 1
                for t in range(NT - GT):
                    tt = slice(t * P, t * P + P)
                    for n, (w, v) in enumerate(((w_hi, v_hi), (w_hi, v_lo), (w_lo, v_hi))):
                        for half in range(2):
                            mm = pe.matmul(y_bank[t][half][:, :], w[:, q, tt], v[:, q, half * 512:half * 512 + 512],
                                           start=(first and n == 0), stop=(last and n == 2))
                mm.then_inc(s_yv, 1)

            def both(i, c):
                v_chunk(i, c)
                a_chunk(i + AHEAD, c)

            chunk_loop(pe, both, (1, 15))

        def taken(eng, key):
            b, n = turn[key]
            eng.wait_ge(full[b], n)
            return bank[b]

        def emptied(eng, key):
            b, n = turn[key]
            eng.wait_ge(free[b], n)

        def half_used(eng, n):
            if n < 3:
                eng.wait_ge(s_modu, n + 1)
            else:
                taken(eng, "mod_cols" if n == 3 else ("row", n))

        def freeing(key):
            return free[turn[key][0]]

        def pv_done(eng, J):
            i, j = JOBS[J]
            if j % 8 == 7:
                taken(eng, ("o", i, j // 8))
            else:
                eng.wait_ge(s_pv, J + 1 - (J + 1) // 8)

        def map_bufs_free(eng, m):
            if m >= 4:
                J = max(a for a in range(N) if first_map[a] <= m - 4)
                taken(eng, ("pT", J))

        @block.sync
        def _(sp):
            def ada(n):
                s, b = ADA_HALVES[n]
                if n >= 2:
                    sp.wait_ge(s_accd, n - 1)
                    half_used(sp, n - 2)
                dst = ring_a[:, 4 * (n % 2):4 * (n % 2) + 4, :].rearrange("p a b -> p (a b)")
                at = s * D + b * 512
                sp.dma_start(dst.rearrange("p (k c) -> p k c", k=KD),
                             w_ada[:, at:at + 512].rearrange("(k p) c -> p k c", p=P)).then_inc(s_ada[n % 2], 16)
                sp.dma_start(b_half[0:1, n % 2, :], b_ada[0:1, at:at + 512]).then_inc(s_ada[n % 2], 16)

            def win(e):
                if e >= 8:
                    b, n = turn[("qk", e - 8)]
                    sp.wait_ge(full[b], n)
                sp.dma_start(ring_w[:, e % 8, :], w_in[e]).then_inc(s_win[e % 8], 16)

            sp.dma_start(x_sb[:, :, :], x[0].rearrange("(t p) d -> p t d", p=P)).then_inc(s_x, 16)
            for n in range(4):
                ada(n)
            for e in range(8):
                win(e)
                if e >= 4:
                    ada(e)
            for e in range(8, IN_TILES):
                win(e)
                if e < 12:
                    ada(e)
            for i in (2, 3):
                b, n = turn[("v", 2, i)]
                sp.wait_ge(full[b], n)
            sp.dma_start(w_outs[:, :, :], w_out.rearrange("(k p) d -> p k d", p=P)).then_inc(s_wout, 16)
            sp.dma_start(keys[:, :, :], keys_t).then_inc(s_keys, 16)
            sp.wait_ge(s_accd, 12)
            for e in range(2 * PH):
                if e >= 8:
                    b, n = turn[("q", e - 8)]
                    sp.wait_ge(full[b], n)
                sp.dma_start(ring_a[:, e % 8, :], wq[e]).then_inc(s_wq[e % 8], 16)
            sp.wait_ge(s_x1, NT)
            sp.dma_start(g1_row[:, :], final_row.partition_broadcast(P)).then_inc(s_fin, 16)

            def load_u(i, c):
                if within(i):
                    after(sp, s_ulo, i - 1)
                    sp.dma_start(u_raw[:, c % 2, :], u_t[bass.ds(i, 1)].rearrange("o p d -> p (o d)"))\
                      .then_inc(s_u[c % 2], 16)

            def load_v(i, c):
                if within(i):
                    after(sp, s_vlo, i - 1)
                    sp.dma_start(v_raw[:, c % 2, :], peer_v[bass.ds(i * P, P), :]).then_inc(s_v[c % 2], 16)

            def load_g(q, parity):
                if within(q, NCHUNK // 4 - 1):
                    after(sp, s_pw, 4 * (q - 1))
                    sp.dma_start(g_in[:, parity, :, :, :].rearrange("p b i t -> p b (i t)"),
                                 gates[:, :, bass.ds(4 * q, 4), :].rearrange("b p i t -> p b (i t)"))\
                      .then_inc(s_g[parity], 16)

            for e in (13, 14, 15):
                b, n = turn[("q", e)]
                sp.wait_ge(full[b], n)
            for i in range(AHEAD + 2):
                load_u(i, i)

            for tile in range(NT - GT):
                def store_gates(tb, parity):
                    sp.wait_ge(s_gt, (tb + 1) * (GB // 4))
                    sp.dma_start(gates[bass.ds(tb, 1)].rearrange("o p i t -> p (o i t)"),
                                 g_out[parity][:, :, :].rearrange("p i t -> p (i t)")).then_inc(s_gst[parity], 16)

                gate_blocks(sp, tile, store_gates)
            for parity in range(2):
                sp.wait_ge(s_gst[parity], 16 * (DT // GB // 2))
            sp.wait_ge(s_idx, NT)
            for q in range(2):
                load_g(q, q)
                load_v(q, q)

            def loads(i, c):
                load_v(i + 2, c)
                load_u(i + AHEAD + 2, c)
                if c % 4 == 3:
                    load_g(over(i, c, 4) + 2, c // 4)

            chunk_loop(sp, loads)
            for i in range(NT):
                sp.wait_ge(s_res, i + 1)
                sp.dma_start(out[0, i * P:i * P + P, :], x_sb[:, i, :]).then_inc(s_out, 16)
            sp.wait_ge(s_out, 16 * NT)

        @block.gpsimd
        def _(pool):
            pool.memset(ident[:, :], 0.0).then_inc(s_const, 1)
            pool.memset(ones[:, :], 1.0).then_inc(s_const, 1)
            pool.iota(ndist[:, :], [[1, S]], base=-(S - P), channel_multiplier=-1,
                      allow_small_or_imprecise_dtypes=True).then_inc(s_const, 1)
            pool.iota(iota16[:, :], [[1, TOPK]], base=0, channel_multiplier=0,
                      allow_small_or_imprecise_dtypes=True).then_inc(s_const, 1)
            pool.iota(iota_k[:, :], [[1, NKEYS]], base=0, channel_multiplier=0,
                      allow_small_or_imprecise_dtypes=True).then_inc(s_const, 1)
            pool.wait_ge(s_const, 5)
            pool.affine_select(out=ident[:, :], in_=ident[:, :], compare_op=ALU.not_equal, fill=1.0, base=0,
                               pattern=[[-1, P]], channel_multiplier=1).then_inc(s_const, 1)
            pool.affine_select(out=ndist[:, :], in_=ndist[:, :], compare_op=ALU.is_ge, fill=MASKED, base=S - P,
                               pattern=[[-1, S]], channel_multiplier=1).then_inc(s_const, 1)
            pool.wait_ge(s_const, 7)
            pool.affine_select(out=ndist_w[:, :], in_=ndist[:, 2 * P:4 * P], compare_op=ALU.is_ge, fill=MASKED,
                               base=-1, pattern=[[1, 2 * P]], channel_multiplier=-1).then_inc(s_const, 1)

            for k in range(KD):
                emptied(pool, ("h2T", k))
                pool.wait_ge(s_hhi, k + 1)
                pool.tensor_tensor(h_lo[:, k, :], hT[:, k, GT * P:S], h_hi[:, k, :].bitcast(f32), ALU.subtract)\
                    .then_inc(s_hlo, 1)

            def split_u(i, c):
                if not within(i):
                    return
                pool.wait_ge(s_uhi, i + 1)
                pool.tensor_tensor(u_lo[:, c % 2, :], u_raw[:, c % 2, :], u_hi[:, c % 2, :].bitcast(f32),
                                   ALU.subtract).then_inc(s_ulo, 1)

            for i in range(AHEAD):
                split_u(i, i)

            for tile in range(NT - GT):
                emptied(pool, ("cols", tile))

                def hot_second(tb, parity):
                    for b in range(GB // 4):
                        B = tb * (GB // 4) + b
                        after(pool, s_gm, B - 1)
                        pool.sem_inc(s_clear, 1)
                        pool.tensor_copy(four[:, b % 2, :], cols[:, 1, bass.ds(tb * GB + 4 * b, 4)]).then_inc(s_four, 1)
                        pool.wait_ge(s_four, B + 1)
                        pool.sem_inc(s_clear, 1)
                        for tok in range(4):
                            ins = pool.tensor_scalar(hot_j[:, b % 2, tok, :], iota_k[:, :],
                                                     four[:, b % 2, tok:tok + 1], None, ALU.is_equal)
                        ins.then_inc(s_j, 1)

                gate_blocks(pool, tile, hot_second)

            def gather(n, c):
                if not within(n):
                    return
                if not isinstance(n, int) or n >= 4:
                    pool.wait_ge(s_dot, n - 3)
                    pool.sem_inc(s_clear, 1)
                    pool.wait_ge(s_acc, n - 3)
                    pool.sem_inc(s_clear, 1)
                pool.tensor_copy(stage[:, c % 4:c % 4 + 1], eidx[:, bass.ds(n, 1)]).then_inc(s_stg, 1)
                pool.wait_ge(s_stg, n + 1)
                pool.sem_inc(s_clear, 1)
                for table, slot in ((peer_u, 2 * (c % 4)), (peer_v, 2 * (c % 4) + 1)):
                    pool.indirect_dma_start(rows[slot][:, :], None, table[:, :],
                                            bass.IndirectOffsetOnAxis(stage[:, c % 4:c % 4 + 1], 0))\
                        .then_inc(s_got[slot], 16)

            pool.wait_ge(s_idx, NT)
            for parity in range(2):
                pool.wait_ge(s_gst[parity], 16 * (DT // GB // 2))
            gather(0, 0)
            gather(1, 1)

            def split_and_gather(i, c):
                split_u(i + AHEAD, c)
                gather(i + 2, c + 2)

            chunk_loop(pool, split_and_gather)

        @block.scalar
        def _(act):
            act.dma_start(c_in[:, :], c_col).then_inc(s_c, 16)
            act.dma_start(n1_col[:, :], norm1_col).then_inc(s_n1, 16)
            act.dma_start(lam_in[:, :, :].rearrange("p a b -> p (a b)"), lam_vecs.partition_broadcast(P))\
               .then_inc(s_lam, 16)
            act.dma_start(subln[:, :], subln_row.partition_broadcast(P)).then_inc(s_small, 16)
            act.dma_start(sinks[:, :], sinks_row.partition_broadcast(P)).then_inc(s_small, 16)
            act.dma_start(a2_row[:, :], norm2_row.partition_broadcast(P)).then_inc(s_small, 16)
            act.wait_ge(s_c, 16)
            act.activation(c_tmp[:, :], c_in[:, :], ACT.Exp, scale=-1.0).then_inc(s_ce, 1)
            act.wait_ge(s_lp, 1)
            act.activation(lam_s[:, 2:4], lam_s[:, 0:2], ACT.Exp).then_inc(s_le, 1)
            act.wait_ge(s_x, 16)
            for i in range(NT):
                act.activation(xn[:, i, :], x_sb[:, i, :], ACT.Square, accum_out=ss[:, i:i + 1]).then_inc(s_ss, 1)
            act.wait_ge(s_ms, 1)
            act.activation(rstd[:, 0:NT], ss[:, 0:NT], ACT.Sqrt).then_inc(s_std, 1)
            emptied(act, "mod_cols")
            for k in range(KD):
                ps = taken(act, ("xT", k))
                act.activation(hT[:, k, :], ps[:, :], ACT.Identity, scale=a1_col[:, k:k + 1],
                               bias=sh1_col[:, k:k + 1]).then_inc(freeing(("xT", k)), 1)
            for e in range(QK_TILES):
                ps = taken(act, ("qk", e))
                act.activation(qkT[:, e, :], ps[:, :], ACT.Copy).then_inc(freeing(("qk", e)), 1)

            def exps(J):
                i, j = JOBS[J]
                kind, maps, scale, _, _, c = plan[j]
                n = len(key_tiles(i, j)) * P
                for m in range(first_map[J], first_map[J] + len(maps)):
                    act.wait_ge(s_nm, m + 1)
                    act.activation(Sb[:, m % 4, 0:n], Sb[:, m % 4, 0:n], ACT.Exp, scale=scale,
                                   bias=nmax[:, m:m + 1], accum_out=den[:, m:m + 1]).then_inc(s_exp, 1)
                if kind == "C":
                    a = i * NCH + c
                    act.activation(esink[:, a:a + 1], sinks[:, c:c + 1], ACT.Exp,
                                   bias=nmax[:, m:m + 1]).then_inc(s_es, 1)

            def take_pT(J):
                n = len(key_tiles(*JOBS[J])) * P
                ps = taken(act, ("pT", J))
                if J >= 2:
                    pv_done(act, J - 2)
                act.activation(pT[:, J % 2, 0:n], ps[:, 0:n], ACT.Copy).then_inc(freeing(("pT", J)), 1)

            for J in range(N + 5):
                if J < N:
                    exps(J)
                if 1 <= J <= N:
                    take_pT(J - 1)
                if J >= 2 and (J - 2) % NHEADS == NHEADS - 1:
                    i = (J - 2) // NHEADS
                    act.wait_ge(s_sso, i + 1)
                    act.activation(sso[:, i, :, 1], sso[:, i, :, 0], ACT.Sqrt).then_inc(s_so, 1)
                if J >= 5 and (J - 5) % NHEADS == NHEADS - 1:
                    i = (J - 5) // NHEADS
                    for half in range(2):
                        ps = taken(act, ("oT", i, half))
                        if i >= 1 and half == 0:
                            taken(act, ("y", i - 1, 1))
                        act.activation(oT[half][:, :, :], ps[:, :].rearrange("p (a b) -> p a b", b=P),
                                       ACT.Copy).then_inc(freeing(("oT", i, half)), 1)

            act.wait_ge(s_ms, 2)
            act.activation(rstd[:, NT:2 * NT], ss[:, NT:2 * NT], ACT.Sqrt).then_inc(s_std, 1)
            for k in range(KD):
                ps = taken(act, ("h2T", k))
                act.activation(hT[:, k, :], ps[:, :], ACT.Copy).then_inc(freeing(("h2T", k)), 1)
                taken(act, ("y", NT - 1, 1))
                emptied(act, ("h2T", k))
                act.activation(h_hi[:, k, :], hT[:, k, GT * P:S], ACT.Copy).then_inc(s_hhi, 1)

            def take_scores(g):
                for i in range(NT):
                    ps = taken(act, ("sc", g, i))
                    n = g * NT + i
                    if n >= 8:
                        act.wait_ge(s_scu, n - 7)
                    act.activation(sc[:, n % 8, :], ps[:, :], ACT.Copy).then_inc(freeing(("sc", g, i)), 1)

            for e in range(2 * PH):
                ps = taken(act, ("q", e))
                if e >= 3:
                    last = e - 3
                    if last % 4 == 3:
                        taken(act, ("sc", last // 4, NT - 1))
                    else:
                        act.wait_ge(s_qTu, last + 1 - (last + 1) // 4)
                act.activation(qT[:, e % 3, :], ps[:, :], ACT.Copy).then_inc(freeing(("q", e)), 1)
                if e % 4 == 0 and e:
                    take_scores(e // 4 - 1)
            take_scores(3)

            def u_high(i, c):
                if not within(i):
                    return
                after(act, s_a, i - 1)
                act.wait_ge(s_u[c % 2], 16 * (over(i, c, 2) + 1))
                act.activation(u_hi[:, c % 2, :], u_raw[:, c % 2, :], ACT.Copy).then_inc(s_uhi, 1)

            def v_high(i, c):
                if not within(i):
                    return
                after(act, s_yv, i - 1)
                act.wait_ge(s_v[c % 2], 16 * (over(i, c, 2) + 1))
                act.activation(v_hi[:, c % 2, :], v_raw[:, c % 2, :], ACT.Copy).then_inc(s_vhi, 1)

            def gelu(i, c):
                if not within(i):
                    return
                after(act, s_pw, i - AHEAD + 1)
                act.wait_ge(s_a, i + 1)
                act.activation(a_act[:, c % AHEAD, :], bank[f"O{c % 2}"][:, 0:DT], ACT.Gelu).then_inc(s_gelu, 1)

            u_high(0, 0)
            for i in range(AHEAD):
                u_high(i + 1, i + 1)
                gelu(i, i)
            for tile in range(NT - GT):
                act.wait_ge(s_gd, tile + 1)
                act.activation(gate[:, tile + GT, :], gate[:, tile + GT, :], ACT.Exp).then_inc(s_ge, 1)

                def take_gates(tb, parity):
                    for b in range(GB // 4):
                        B = tb * (GB // 4) + b
                        if b == 0:
                            after(act, s_gst[parity], 16 * over(tb, parity, 2))
                        act.wait_ge(s_gm, B + 1)
                        act.activation(g_out[parity][:, :, 4 * b:4 * b + 4].rearrange("p i t -> p t i"),
                                       bank[f"T{b % 2}"][:, :].rearrange("p (t i) -> p t i", t=4), ACT.Copy)\
                           .then_inc(s_gt, 1)

                gate_blocks(act, tile, take_gates)
            for tile in range(GT):
                act.wait_ge(s_gd, NT)
                act.activation(gate[:, tile, :], gate[:, tile, :], ACT.Exp).then_inc(s_ge, 1)
            for parity in range(2):
                act.wait_ge(s_gst[parity], 16 * (DT // GB // 2))
            v_high(0, 0)

            def parts(i, c):
                v_high(i + 1, c + 1)
                u_high(i + AHEAD + 1, c + 1)
                gelu(i + AHEAD, c)
                act.wait_ge(s_dot, i + 1)
                after(act, s_wgt, i - 1)
                act.activation(act_g[:, c % 2:c % 2 + 1], dots[:, c % 2:c % 2 + 1], ACT.Gelu).then_inc(s_dgelu, 1)

            chunk_loop(act, parts)
            act.wait_ge(s_f2, 1)
            act.activation(rstd[:, 2 * NT:3 * NT], ss[:, 2 * NT:3 * NT], ACT.Sqrt).then_inc(s_fs, 1)

        @block.vector
        def _(dve):
            def bcast(ap, shape):
                return ap.to_broadcast(shape)

            dve.wait_ge(s_ce, 1)
            done(dve, dve.tensor_scalar(c_tmp[:, :], c_tmp[:, :], 1.0, None, ALU.add), s_dv)
            done(dve, dve.reciprocal(c_tmp[:, :], c_tmp[:, :]), s_dv)
            done(dve, dve.tensor_tensor(c_silu[:, :], c_in[:, :], c_tmp[:, :], ALU.mult), s_dv)
            dve.wait_ge(s_lam, 16)
            done(dve, dve.tensor_tensor(lam_prod[:, :, :], lam_in[:, 0:4:2, :], lam_in[:, 1:4:2, :], ALU.mult), s_dv)
            dve.tensor_reduce(lam_s[:, 0:2], lam_prod[:, :, :], AX, ALU.add).then_inc(s_lp, 1)
            dve.wait_ge(s_le, 1)
            done(dve, dve.tensor_tensor(lam_s[:, 4:5], lam_s[:, 3:4], lam_s[:, 2:3], ALU.subtract), s_dv)
            done(dve, dve.tensor_scalar(lam_s[:, 5:6], lam_s[:, 4:5], -LAM_INIT, None, ALU.add), s_dv)
            dve.wait_ge(s_small, 48)
            done(dve, dve.tensor_scalar(subln[:, :], subln[:, :], 1.0 - LAM_INIT, None, ALU.mult), s_dv)
            done(dve, dve.tensor_scalar(nsinks[:, :], sinks[:, :], -1.0, None, ALU.mult), s_dv)
            dve.wait_ge(s_ss, NT)
            dve.tensor_scalar(ss[:, 0:NT], ss[:, 0:NT], 1.0 / D, EPS, ALU.mult, ALU.add).then_inc(s_ms, 1)
            dve.wait_ge(s_std, 1)
            done(dve, dve.reciprocal(rstd[:, 0:NT], rstd[:, 0:NT]), s_dv)
            for i in range(NT):
                dve.tensor_scalar(xn[:, i, :], x_sb[:, i, :], rstd[:, i:i + 1], None, ALU.mult).then_inc(s_xn, 1)

            def mod_half(n):
                acc = mod_acc[:, n % 2, :]
                w = ring_a[:, 4 * (n % 2):4 * (n % 2) + 4, :].rearrange("p a b -> p (a b)")\
                    .rearrange("p (k c) -> p k c", k=KD)
                if n >= 2:
                    half_used(dve, n - 2)
                dve.wait_ge(s_ada[n % 2], 32 * (n // 2 + 1))
                done(dve, dve.tensor_scalar(acc, w[:, 0, :], c_silu[:, 0:1], None, ALU.mult), s_dv)
                for k in range(1, KD):
                    ins = dve.scalar_tensor_tensor(out=acc, in0=w[:, k, :], scalar=c_silu[:, k:k + 1], in1=acc,
                                                   op0=ALU.mult, op1=ALU.add)
                    if k < KD - 1:
                        done(dve, ins, s_dv)
                    else:
                        ins.then_inc(s_accd, 1)

            def mod_row(n):
                ps = taken(dve, ("row", n))
                dst = {2: g1_row, 4: a2_row, 3: sh2_row, 5: g2_row}[ADA_HALVES[n][0]]
                at = slice(512 * ADA_HALVES[n][1], 512 * ADA_HALVES[n][1] + 512)
                if ADA_HALVES[n][0] == 4:
                    ins = dve.scalar_tensor_tensor(out=dst[:, at], in0=ps[:, :], scalar=1.0, in1=dst[:, at],
                                                   op0=ALU.add, op1=ALU.mult)
                else:
                    ins = dve.tensor_copy(dst[:, at], ps[:, :])
                ins.then_inc(freeing(("row", n)), 1)

            for n in range(4):
                mod_half(n)
            mcols = taken(dve, "mod_cols")
            dve.wait_ge(s_n1, 16)
            done(dve, dve.scalar_tensor_tensor(out=a1_col[:, :], in0=mcols[:, 0:8], scalar=1.0, in1=n1_col[:, :],
                                               op0=ALU.add, op1=ALU.mult), s_dv)
            dve.tensor_copy(sh1_col[:, :], mcols[:, 8:16]).then_inc(freeing("mod_cols"), 1)
            mod_half(4)
            for n in range(5, 12):
                mod_half(n)
                mod_row(n - 1)
            mod_row(11)
            emptied(dve, ("row", 11))
            for n in range(V_COLS // 256):
                for i in range(NT):
                    ps = taken(dve, ("v", n, i))
                    dve.tensor_copy(v_sb[:, i, 256 * n:256 * n + 256], ps[:, 0:256]).then_inc(freeing(("v", n, i)), 1)

            dve.wait_ge(s_const, 8)

            def soft_in(J):
                i, j = JOBS[J]
                kind, maps, scale, slope, _, c = plan[j]
                n = len(key_tiles(i, j)) * P
                nd = ndist_w[:, 2 * P - n:2 * P] if kind == "C" else ndist[:, S - n:S]
                for m in range(first_map[J], first_map[J] + len(maps)):
                    ps = taken(dve, ("s", m))
                    map_bufs_free(dve, m)
                    dve.scalar_tensor_tensor(out=Sb[:, m % 4, 0:n], in0=nd, scalar=slope / scale, in1=ps[:, 0:n],
                                             op0=ALU.mult, op1=ALU.add).then_inc(freeing(("s", m)), 1)
                    emptied(dve, ("s", m))
                    done(dve, dve.tensor_reduce(mx[:, m:m + 1], Sb[:, m % 4, 0:n], AX, ALU.max), s_dv)
                    if kind == "C":
                        dve.tensor_scalar(nmax[:, m:m + 1], mx[:, m:m + 1], -scale, nsinks[:, c:c + 1],
                                          ALU.mult, ALU.min).then_inc(s_nm, 1)
                    else:
                        dve.tensor_scalar(nmax[:, m:m + 1], mx[:, m:m + 1], -scale, None, ALU.mult).then_inc(s_nm, 1)

            def post(J):
                i, j = JOBS[J]
                kind, maps, _, _, _, c = plan[j]
                m = first_map[J]
                dve.wait_ge(s_exp, m + len(maps))
                if kind == "A":
                    r = ra[:, i * NA + j, :]
                    done(dve, dve.reciprocal(r, den[:, m:m + 2]), s_dv)
                    done(dve, dve.tensor_tensor(r[:, 1:2], r[:, 1:2], lam_s[:, 5:6], ALU.mult), s_dv)
                    n = len(key_tiles(i, j)) * P
                    one, two = Sb[:, m % 4, 0:n], Sb[:, (m + 1) % 4, 0:n]
                    done(dve, dve.tensor_scalar(one, one, r[:, 0:1], None, ALU.mult), s_dv)
                    dve.scalar_tensor_tensor(out=one, in0=two, scalar=r[:, 1:2], in1=one,
                                             op0=ALU.mult, op1=ALU.add).then_inc(s_comb, 1)
                    return
                if kind == "C":
                    a = i * NCH + c
                    dve.wait_ge(s_es, a + 1)
                    done(dve, dve.tensor_tensor(den[:, m:m + 1], den[:, m:m + 1], esink[:, a:a + 1], ALU.add), s_dv)
                done(dve, dve.reciprocal(rden[:, i, j:j + 1], den[:, m:m + 1]), s_dv)

            def heads_out(i):
                taken(dve, ("o", i, 0))
                taken(dve, ("o", i, 1))
                if i:
                    taken(dve, ("oT", i - 1, 1))
                nA = NA * HD
                oa = o_sb[:, 0:nA]
                done(dve, dve.tensor_copy(oa, bank["O0"][:, 0:nA]), s_dv)
                done(dve, dve.tensor_tensor(rep[:, 0:nA], oa, oa, ALU.mult), s_dv)
                done(dve, dve.tensor_reduce(sso[:, i, :, 0], rep[:, 0:nA].rearrange("p (h d) -> p h d", d=HD),
                                            AX, ALU.add), s_dv)
                dve.tensor_scalar(sso[:, i, :, 0], sso[:, i, :, 0], 1.0 / HD, EPS, ALU.mult, ALU.add).then_inc(s_sso, 1)
                for b, lo, hi in (("O0", NA, 8), ("O1", 8, NHEADS)):
                    dve.tensor_tensor(o_sb[:, lo * HD:hi * HD].rearrange("p (h d) -> p h d", d=HD),
                                      bank[b][:, (lo % 8) * HD:512].rearrange("p (h d) -> p h d", d=HD),
                                      rden[:, i, lo:hi].unsqueeze(2).to_broadcast([P, hi - lo, HD]),
                                      ALU.mult).then_inc(free[b], 1)
                dve.wait_ge(s_so, i + 1)
                done(dve, dve.reciprocal(sso[:, i, :, 1], sso[:, i, :, 1]), s_dv)
                o4 = oa.rearrange("p (h d) -> p h d", d=HD)
                done(dve, dve.tensor_tensor(o4, o4, sso[:, i, :, 1].unsqueeze(2).to_broadcast([P, NA, HD]),
                                            ALU.mult), s_dv)
                dve.tensor_tensor(o4, o4, subln[:, :].unsqueeze(1).to_broadcast([P, NA, HD]), ALU.mult).then_inc(s_o, 1)

            def add_mixer(i):
                for half in range(2):
                    at = slice(512 * half, 512 * half + 512)
                    ps = taken(dve, ("y", i, half))
                    dve.tensor_tensor(mod_acc[:, half, :], ps[:, :], g1_row[:, at], ALU.mult)\
                       .then_inc(freeing(("y", i, half)), 1)
                    emptied(dve, ("y", i, half))
                    ins = dve.tensor_tensor(x_sb[:, i, at], x_sb[:, i, at], mod_acc[:, half, :], ALU.add)
                    done(dve, ins, s_x1 if half else s_dv)

            for J in range(N + 6):
                if J < N:
                    soft_in(J)
                if 1 <= J <= N:
                    post(J - 1)
                if J >= 2 and (J - 2) % NHEADS == NHEADS - 1:
                    heads_out((J - 2) // NHEADS)
                if J >= 6 and (J - 6) % NHEADS == NHEADS - 1:
                    add_mixer((J - 6) // NHEADS)

            flat = mod_acc[:, :, :].rearrange("p a b -> p (a b)")
            for i in range(NT):
                done(dve, dve.tensor_tensor_reduce(out=flat, in0=x_sb[:, i, :], in1=x_sb[:, i, :], scale=1.0,
                                                   scalar=0.0, op0=ALU.mult, op1=ALU.add,
                                                   accum_out=ss[:, NT + i:NT + i + 1]), s_dv)
            dve.tensor_scalar(ss[:, NT:2 * NT], ss[:, NT:2 * NT], 1.0 / D, EPS, ALU.mult, ALU.add).then_inc(s_ms, 1)
            dve.wait_ge(s_std, 2)
            done(dve, dve.reciprocal(rstd[:, NT:2 * NT], rstd[:, NT:2 * NT]), s_dv)
            for i in range(NT):
                done(dve, dve.scalar_tensor_tensor(out=h2[:, i, :], in0=x_sb[:, i, :], scalar=rstd[:, NT + i:NT + i + 1],
                                                   in1=a2_row[:, :], op0=ALU.mult, op1=ALU.mult), s_dv)
                dve.tensor_tensor(h2[:, i, :], h2[:, i, :], sh2_row[:, :], ALU.add).then_inc(s_h2, 1)
            dve.wait_ge(s_h2, NT)

            def best16(src, values, places, copy):
                step = s_dv
                for a, v in zip(src, values):
                    last = dve.max(v[:, 0:8], a)
                    if a is not src[-1]:
                        last.then_inc(step, 1)
                        tally[step.name] += 1
                done(dve, last, step)
                for a, v, q, t in zip(src, values, places, copy):
                    dve.max_index(q[:, 0:8], v[:, 0:8], a)
                    last = dve.match_replace(t, v[:, 0:8], a, -3.0e38)
                    if a is not src[-1]:
                        last.then_inc(step, 1)
                        tally[step.name] += 1
                done(dve, last, step)
                for t, v in zip(copy, values):
                    last = dve.max(v[:, 8:16], t)
                    if t is not copy[-1]:
                        last.then_inc(step, 1)
                        tally[step.name] += 1
                done(dve, last, step)
                for t, v, q in zip(copy, values, places):
                    last = dve.max_index(q[:, 8:16], v[:, 8:16], t)
                    if t is not copy[-1]:
                        last.then_inc(step, 1)
                        tally[step.name] += 1
                done(dve, last, step)

            for g in range(4):
                for i in range(NT):
                    n = g * NT + i
                    emptied(dve, ("sc", g, i))
                    heads = [(2 * g + a, s) for a in range(2) for s in range(2)]
                    best16([sc[:, n % 8, P * q:P * q + P] for q in range(4)],
                           [sv[:, i, h, s, :] for h, s in heads], [si[:, i, h, s, :] for h, s in heads],
                           [rep[:, P * q:P * q + P] for q in range(4)])
                    for a in range(2):
                        h = 2 * g + a
                        ins = dve.tensor_tensor(cand[:, a, :, :],
                                                sv[:, i, h, 0, :].unsqueeze(2).to_broadcast([P, TOPK, TOPK]),
                                                sv[:, i, h, 1, :].unsqueeze(1).to_broadcast([P, TOPK, TOPK]), ALU.add)
                        if a:
                            ins.then_inc(s_scu, 1)
                    dve.wait_ge(s_scu, n + 1)
                    best16([cand[:, a, :, :].rearrange("p a b -> p (a b)") for a in range(2)],
                           [topv[:, i, 2 * g + a, :] for a in range(2)], [topp[:, i, 2 * g + a, :] for a in range(2)],
                           [rep[:, 256 * a:256 * a + 256] for a in range(2)])

            HK = PH * TOPK

            def decode(i):
                pos = topp[:, i, :, :].rearrange("p h k -> p (h k)")
                done(dve, dve.tensor_scalar(side_u[:, 0, :], pos, 4, None, ALU.logical_shift_right), s_dv)
                done(dve, dve.tensor_scalar(side_u[:, 1, :], pos, 15, None, ALU.bitwise_and), s_dv)
                done(dve, dve.tensor_copy(side_f[:, :, :], side_u[:, :, :]), s_dv)
                done(dve, dve.tensor_copy(sif[:, :, :, :], si[:, i, :, :, :]), s_dv)
                for s in range(2):
                    hot = onehot.rearrange("p (a b) -> p a b", b=TOPK)
                    done(dve, dve.tensor_tensor(hot, iota16[:, :].unsqueeze(1).to_broadcast([P, HK, TOPK]),
                                                side_f[:, s, :].unsqueeze(2).to_broadcast([P, HK, TOPK]),
                                                ALU.is_equal), s_dv)
                    for h in range(PH):
                        hot = onehot.rearrange("p (h k a) -> p h k a", k=TOPK, a=TOPK)[:, h, :, :]
                        ins = dve.tensor_tensor(hot, hot, sif[:, h, s, :].unsqueeze(1).to_broadcast([P, TOPK, TOPK]),
                                                ALU.mult)
                        tally[s_dv.name] += 1
                        ins.then_inc(s_dv, 1)
                    dve.wait_ge(s_dv, tally[s_dv.name])
                    done(dve, dve.tensor_reduce(key_f[:, i, s, :], onehot.rearrange("p (a b) -> p a b", b=TOPK),
                                                AX, ALU.add), s_dv)
                if i < GT:
                    done(dve, dve.scalar_tensor_tensor(out=eidx[:, :], in0=key_f[:, i, 0, :], scalar=float(NKEYS),
                                                       in1=key_f[:, i, 1, :], op0=ALU.mult, op1=ALU.add), s_dv)
                gt = gate[:, i, :].rearrange("p (h k) -> p h k", k=TOPK)
                done(dve, dve.tensor_tensor(gt, topv[:, i, :, :], topv[:, i, :, 0:1].to_broadcast([P, PH, TOPK]),
                                            ALU.subtract), s_gd)
                dve.wait_ge(s_ge, tally[s_gd.name])
                done(dve, dve.tensor_reduce(gsum[:, :], gt, AX, ALU.add), s_dv)
                done(dve, dve.reciprocal(gsum[:, :], gsum[:, :]), s_dv)
                done(dve, dve.tensor_tensor(gt, gt, gsum[:, :].unsqueeze(2).to_broadcast([P, PH, TOPK]),
                                            ALU.mult), s_idx)

            emptied(dve, ("h2T", KD - 1))
            for k in range(KD):
                dve.wait_ge(s_hlo, k + 1)
            for tile in range(NT - GT):
                decode(tile + GT)
                ps = taken(dve, ("cols", tile))
                dve.tensor_copy(cols[:, :, tile * P:tile * P + P], ps[:, 0:3 * P].rearrange("p (a b) -> p a b", b=P))\
                   .then_inc(freeing(("cols", tile)), 1)
                emptied(dve, ("cols", tile))

                def hot_first(tb, parity):
                    for b in range(GB // 4):
                        B = tb * (GB // 4) + b
                        after(dve, s_gm, B - 1)
                        for tok in range(4):
                            n = tb * GB + 4 * b + tok
                            ins = dve.tensor_scalar(hot_i[:, b % 2, tok, :], iota_k[:, :], cols[:, 0, bass.ds(n, 1)],
                                                    cols[:, 2, bass.ds(n, 1)], ALU.is_equal, ALU.mult)
                        ins.then_inc(s_i, 1)

                gate_blocks(dve, tile, hot_first)
            for tile in range(GT):
                decode(tile)
            done(dve, dve.memset(y0[:, :], 0.0), s_dv)
            dve.wait_ge(s_gm, DT // 4)
            for parity in range(2):
                dve.wait_ge(s_gst[parity], 16 * (DT // GB // 2))

            def weigh(i, c):
                dve.wait_ge(s_g[(c // 4) % 2], 16 * (over(i, c, 8) + 1))
                dve.wait_ge(s_gelu, i + 1)
                dve.tensor_tensor(w_f[:, :].rearrange("p (b t) -> p b t", t=GB),
                                  a_act[:, c, :].rearrange("p (b t) -> p b t", t=GB),
                                  g_in[:, (c // 4) % 2, :, c % 4, :], ALU.mult).then_inc(s_pw, 1)
                dve.wait_ge(s_pw, i + 1)
                after(dve, s_yv, i - 1)
                dve.tensor_copy(w_hi[:, c % 2, :], w_f[:, :]).then_inc(s_whi, 1)
                dve.wait_ge(s_whi, i + 1)
                dve.tensor_tensor(w_lo[:, c % 2, :], w_f[:, :], w_hi[:, c % 2, :].bitcast(f32), ALU.subtract)\
                   .then_inc(s_w, 1)
                dve.wait_ge(s_w, i + 1)

            def row_sum(n, c):
                q = slice(c % 2, c % 2 + 1)
                dve.wait_ge(s_dgelu, n + 1)
                dve.tensor_tensor(wgt[:, q], act_g[:, q], gate[:, 0, bass.ds(n, 1)], ALU.mult).then_inc(s_wgt, 1)
                dve.wait_ge(s_wgt, n + 1)
                after(dve, s_acc, n)
                dve.wait_ge(s_got[2 * (c % 4) + 1], 16 * (over(n, c, 4) + 1))
                dve.scalar_tensor_tensor(out=y0[:, :], in0=rows[2 * (c % 4) + 1][:, :], scalar=wgt[:, q], in1=y0[:, :],
                                         op0=ALU.mult, op1=ALU.add).then_inc(s_acc, 1)

            def chunk(i, c):
                weigh(i, c)
                dve.wait_ge(s_vhi, i + 1)
                dve.tensor_tensor(v_lo[:, c % 2, :], v_raw[:, c % 2, :], v_hi[:, c % 2, :].bitcast(f32), ALU.subtract)\
                   .then_inc(s_vlo, 1)
                after(dve, s_dot, i)
                dve.wait_ge(s_got[2 * (c % 4)], 16 * (over(i, c, 4) + 1))
                dve.scalar_tensor_tensor(out=junk[:, :], in0=rows[2 * (c % 4)][:, :], scalar=1.0, in1=h2[:, 0, :],
                                         op0=ALU.mult, op1=ALU.mult, accum_out=dots[:, c % 2:c % 2 + 1])\
                   .then_inc(s_dot, 1)
                if not isinstance(i, int) or i:
                    row_sum(i - 1, c - 1 if c else AHEAD - 1)

            chunk_loop(dve, chunk)
            row_sum(NCHUNK - 1, AHEAD - 1)

            dve.wait_ge(s_acc, NCHUNK)
            dve.wait_ge(s_yv, NCHUNK)
            dve.wait_ge(s_fin, 16)
            done(dve, dve.tensor_tensor(y0[:, :], y0[:, :], g2_row[:, :], ALU.mult), s_dv)
            done(dve, dve.tensor_tensor(x_sb[:, 0, :], x_sb[:, 0, :], y0[:, :], ALU.add), s_dv)
            for i in range(GT, NT):
                for half in range(2):
                    part = slice(512 * half, 512 * half + 512)
                    done(dve, dve.tensor_tensor(mod_acc[:, half, :], y_bank[i - GT][half][:, :], g2_row[:, part],
                                                ALU.mult), s_dv)
                    done(dve, dve.tensor_tensor(x_sb[:, i, part], x_sb[:, i, part], mod_acc[:, half, :], ALU.add), s_dv)
            for i in range(NT):
                done(dve, dve.tensor_tensor_reduce(out=flat, in0=x_sb[:, i, :], in1=x_sb[:, i, :], scale=1.0,
                                                   scalar=0.0, op0=ALU.mult, op1=ALU.add,
                                                   accum_out=ss[:, 2 * NT + i:2 * NT + i + 1]), s_dv)
            last = slice(2 * NT, 3 * NT)
            dve.tensor_scalar(ss[:, last], ss[:, last], 1.0 / D, EPS, ALU.mult, ALU.add).then_inc(s_f2, 1)
            dve.wait_ge(s_fs, 1)
            done(dve, dve.reciprocal(rstd[:, last], rstd[:, last]), s_dv)
            for i in range(NT):
                dve.scalar_tensor_tensor(out=x_sb[:, i, :], in0=x_sb[:, i, :], scalar=rstd[:, 2 * NT + i:2 * NT + i + 1],
                                         in1=g1_row[:, :], op0=ALU.mult, op1=ALU.mult).then_inc(s_res, 1)


def kernel(**inputs):
    import concourse.bacc as bacc
    from concourse.bass_utils import run_bass_kernel_spmd as run

    a = {n: np.asarray(v) for n, v in inputs.items()}
    qa, ka, va, qb, kb, vb, qc, kc, vc = np.split(
        np.arange(a["w_in"].shape[2]), np.cumsum([256, 256, 256, 384, 384, 384, 384, 128]))
    qc = qc.reshape(2, CG, HD).transpose(1, 0, 2).reshape(-1)
    order = np.concatenate([qa, ka, qb, kb, qc, kc, va, vb, vc])
    w_in = a["w_in"][0][:, order].reshape(KD, P, IN_TILES, P).transpose(2, 1, 0, 3).reshape(IN_TILES, P, D)
    wq = a["peer_wq"][0].reshape(KD, P, 2 * PH, P).transpose(2, 1, 0, 3).reshape(2 * PH, P, D)
    data = {
        "x": a["x"], "c_col": a["c"].reshape(KD, P).T, "norm1_col": a["norm1_g"].reshape(KD, P).T,
        "w_ada": a["w_ada"][0], "b_ada": a["b_ada"], "w_in": w_in, "w_out": a["w_out"][0],
        "lam_vecs": np.concatenate([a[n][0] for n in ("lam_q1", "lam_k1", "lam_q2", "lam_k2")]),
        "subln_row": a["subln_g"][0], "sinks_row": a["sinks"][0], "norm2_row": a["norm2_g"][0], "wq": wq,
        "keys_t": a["peer_keys"][0].transpose(3, 0, 1, 2).reshape(P, 2 * PH, NKEYS),
        "peer_u": a["peer_u"][0], "peer_v": a["peer_v"][0],
        "u_t": a["peer_u"][0].reshape(NCHUNK, P, KD, P).transpose(0, 3, 2, 1).reshape(NCHUNK, P, D),
        "final_row": a["final_g"],
    }
    nc = bacc.Bacc("TRN2", target_bir_lowering=False, num_devices=1)
    arrays, args = {}, []
    for name, v in data.items():
        v = np.ascontiguousarray(v)
        arrays["in_" + name] = v
        args.append(nc.dram_tensor("in_" + name, v.shape, mybir.dt.from_np(v.dtype), kind="ExternalInput").ap())
    args.append(nc.dram_tensor("out_0", (1, S, D), mybir.dt.float32, kind="ExternalOutput").ap())
    peer_block_kernel(nc, *args)
    return run(nc, [arrays], core_ids=[0]).results[0]["out_0"]
```

```python
import numpy as np
import concourse.bass as bass
from concourse import mybir
from contextlib import ExitStack

P = 128
D, S = 1024, 512
KD = D // P
NT = S // P
HD = 64
NA, NB, NCH = 4, 6, 6
CG = NCH // 2
NHEADS = NA + NB + NCH
QK_TILES, V_COLS = 14, 768
IN_TILES = QK_TILES + V_COLS // P
PH, TOPK, NKEYS = 8, 16, 128
NCHUNK = NKEYS
GT = 1
DT = S - GT * P
GB = 32
RING = 6
AHEAD = 8
SPILL = 40
EARLY = SPILL + AHEAD
MAIN = NCHUNK - SPILL
EPS = 1e-6
LAM_INIT = 0.8 - 0.6
MASKED = -1e30
SLOPES = [2.0 ** (-8.0 * n / NHEADS) for n in range(1, NHEADS + 1)]


HEAD_ORDER = "ABCBACBCABCBACBC"


def head_plan():
    kinds = {"A": [], "B": [], "C": []}
    for h in range(NA):
        maps = [(h // 2, 2 + h // 2, 64 * (h % 2) + 32 * m, 32) for m in range(2)]
        kinds["A"].append(("A", maps, 32 ** -0.5, SLOPES[NCH + h], h * HD, h, h))
    for h in range(NB):
        kinds["B"].append(("B", [(4 + h // 2, 7 + h // 2, 64 * (h % 2), 64)], 64 ** -0.5,
                           SLOPES[NCH + NA + h], 256 + h * HD, h, NA + h))
    for h in range(NCH):
        kv = h // CG
        kinds["C"].append(("C", [(10 + h % CG, 13, 64 * kv, 64)], 64 ** -0.5, SLOPES[h], 640 + kv * HD, h, NA + NB + h))
    return [kinds[k].pop(0) for k in HEAD_ORDER]


def peer_block_kernel(nc, x, c_col, norm1_col, w_ada, b_ada, w_in, w_out, lam_vecs, subln_row, sinks_row,
                      norm2_row, wq, keys_t, peer_u, peer_v, u_t, final_row, out):
    f32, u32, f32r = mybir.dt.float32, mybir.dt.uint32, mybir.dt.float32r
    ALU, ACT, AX = mybir.AluOpType, mybir.ActivationFunctionType, mybir.AxisListType.X
    ctx = ExitStack()
    with ctx:
        def sb(name, shape, dt=f32):
            return ctx.enter_context(nc.sbuf_tensor(name, shape, dt))

        def sem(name):
            return ctx.enter_context(nc.semaphore(name))

        base = -(-nc.sbuf_base // 32) * 32
        slab = sb("slab", [P, 184 * 256])

        def at(name, kib, shape, dt=f32):
            return nc.alloc_sbuf_tensor_at(name, shape, dt, offset=base + int(kib * 1024))

        x_sb = at("x_sb", 0, [P, NT, D])
        h2 = at("h2", 16, [P, NT, D])
        hT = at("hT", 32, [P, KD, S])
        ring_w = at("ring_w", 48, [P, 8, D])
        ring_a = at("ring_a", 80, [P, 8, D])
        qkT = at("qkT", 112, [P, QK_TILES, S])
        keys = at("keys", 140, [P, 2 * PH, NKEYS])
        a2_row = at("a2_row", 148, [P, D])
        sh2_row = at("sh2_row", 152, [P, D])
        v_sb = at("v_sb", 156, [P, NT, V_COLS])
        g1_row = at("g1_row", 168, [P, D])
        g2_row = at("g2_row", 172, [P, D])
        mod_acc = at("mod_acc", 176, [P, 2, 512])
        o_sb = at("o_sb", 180, [P, D])
        pT = at("pT", 104, [P, 2, S])
        oT = [at("oT0", 108, [P, 4, P]), at("oT1", 110, [P, 4, P])]
        win_hi = at("win_hi", 64, [P, 2, D], f32r)
        win_lo = at("win_lo", 72, [P, 2, D], f32r)
        h1_hi = at("h1_hi", 16, [P, KD, DT], f32r)
        h1_lo = [at(f"h1_lo{k}", kib, [P, DT], f32r)
                 for k, kib in enumerate((28, 29.5, 140, 141.5, 143, 144.5, 146, 180))]
        a_act = at("a_act", 20, [P, AHEAD, DT])
        y0 = at("y0", 32, [P, D])
        g_in = at("g_in", 36, [P, 2, DT // GB, 4, GB])
        cols = at("cols", 36, [P, 3, DT])
        v_raw = at("v_raw", 48, [P, 2, D])
        h_hi = at("h_hi", 56, [P, KD, DT], f32r)
        h_lo = at("h_lo", 68, [P, KD, DT], f32r)
        wq_hi = at("wq_hi", 96, [P, 2, D], f32r)
        wq_lo = at("wq_lo", 104, [P, 2, D], f32r)
        u_raw = at("u_raw", 80, [P, 2, D])
        u_hi = at("u_hi", 88, [P, 2, D], f32r)
        u_lo = at("u_lo", 96, [P, 2, D], f32r)
        v_hi = at("v_hi", 112, [P, 2, D], f32r)
        v_lo = at("v_lo", 120, [P, 2, D], f32r)
        g_out = [at("g_out0", 112, [P, P, GB]), at("g_out1", 140, [P, P, GB])]
        hot_j = at("hot_j", 128, [P, 2, 4, P])
        hot_i = at("hot_i", 132, [P, 2, 4, P])
        w_f = at("w_f", 128, [P, DT])
        w_hi = at("w_hi", 130, [P, 2, DT], f32r)
        w_lo = at("w_lo", 133, [P, 2, DT], f32r)
        rows = [at(f"row{j}", k, [P, D]) for j, k in enumerate((104, 108, 140, 144, 148, 152, 156, 160,
                                                                     136, 164, 168, 176))]
        fin_row = at("fin_row", 80, [P, D])
        ident = sb("ident", [P, P])
        ones = sb("ones", [P, P])
        ndist = sb("ndist", [P, S])
        ndist_w = sb("ndist_w", [P, 2 * P])
        b_half = sb("b_half", [1, 2, 512])
        c_in = sb("c_in", [P, KD])
        c_silu = sb("c_silu", [P, KD])
        c_tmp = sb("c_tmp", [P, KD])
        n1_col = sb("n1_col", [P, KD])
        a1_col = sb("a1_col", [P, KD])
        sh1_col = sb("sh1_col", [P, KD])
        lam_in = sb("lam_in", [P, 4, 32])
        lam_prod = sb("lam_prod", [P, 2, 32])
        lam_s = sb("lam_s", [P, 8])
        subln = sb("subln", [P, HD])
        sinks = sb("sinks", [P, NCH])
        nsinks = sb("nsinks", [P, NCH])
        ss = sb("ss", [P, 3 * NT])
        rstd = sb("rstd", [P, 3 * NT])
        MAPS = NA + NHEADS
        mx = sb("mx", [P, NT * MAPS])
        nmax = sb("nmax", [P, NT * MAPS])
        den = sb("den", [P, NT * MAPS])
        esink = sb("esink", [P, NT * NCH])
        rden = sb("rden", [P, NT, NHEADS])
        ra = sb("ra", [P, NT * NA, 2])
        sso = sb("sso", [P, NT, NA, 2])
        si = sb("si", [P, NT, PH, 2, TOPK], u32)
        topp = sb("topp", [P, NT, PH, TOPK], u32)
        rep = mod_acc[:, 0, :]
        cand = mod_acc[:, 1, :].rearrange("p (h a b) -> p h a b", a=TOPK, b=TOPK)
        side_u = sb("side_u", [P, 2, PH * TOPK], u32)
        eidx = sb("eidx", [P, PH * TOPK], u32)
        gate = sb("gate", [P, NT, PH * TOPK])
        gsum = sb("gsum", [P, PH])
        iota16 = sb("iota16", [P, TOPK])
        iota_k = sb("iota_k", [P, NKEYS])
        stage = sb("stage", [P, RING], u32)
        dots = sb("dots", [P, 2])
        act_g = sb("act_g", [P, 2])
        wgt = sb("wgt", [P, 2])
        late = v_sb[:, :, :].rearrange("p t c -> p (t c)")
        sv = late[:, 0:1024].rearrange("p (t h s k) -> p t h s k", t=NT, h=PH, s=2)
        topv = late[:, 1024:1536].rearrange("p (t h k) -> p t h k", t=NT, h=PH)
        sif = late[:, 1536:1792].rearrange("p (h s k) -> p h s k", h=PH, s=2)
        side_f = late[:, 1792:2048].rearrange("p (s k) -> p s k", s=2)
        key_f = late[:, 2048:3072].rearrange("p (t s k) -> p t s k", t=NT, s=2)
        xn = qkT[:, 0:8, :].rearrange("p (t a) s -> p t (a s)", t=NT)
        Sb = hT
        junk = o_sb
        w_outs = ring_w
        onehot = ring_w[:, 0:2, :].rearrange("p a b -> p (a b)")
        sc = qkT[:, 0:8, :]
        qT = qkT[:, 8:11, :]

        bank = {n: ctx.enter_context(nc.psum_tensor("bank_" + n, [P, 512], f32))
                for n in ("S0", "S1", "S2", "T0", "T1", "O0", "O1", "G")}
        full = {n: sem("full_" + n) for n in bank}
        free = {n: sem("free_" + n) for n in bank}
        turn = {}
        fillings = dict.fromkeys(bank, 0)

        s_x, s_out = sem("x_loaded"), sem("out_stored")
        s_c, s_n1, s_lam, s_small = sem("c_loaded"), sem("norm1_loaded"), sem("lam_loaded"), sem("rows_loaded")
        s_ada = [sem("ada_loaded0"), sem("ada_loaded1")]
        s_win = [sem(f"w_loaded{j}") for j in range(4)]
        s_inhi, s_inlo = sem("w_in_hi_ready"), sem("w_in_lo_ready")
        s_h1hi, s_h1lo = sem("h1_hi_ready"), sem("h1_lo_ready")
        s_wout, s_keys, s_fin = sem("w_out_loaded"), sem("keys_loaded"), sem("final_loaded")
        s_wq = [sem(f"wq_loaded{j}") for j in range(4)]
        s_qhi, s_qlo = sem("wq_hi_ready"), sem("wq_lo_ready")
        s_const = sem("constants_made")
        s_accd, s_modu, s_rows = sem("mod_summed"), sem("mod_used"), sem("mod_rows_ready")
        s_dv = sem("vector_steps")
        s_ce, s_ss, s_ms, s_std, s_xn = sem("exp_c"), sem("squares"), sem("mean_squares"), sem("std"), sem("xn_ready")
        s_rden = sem("denominators_inverted")
        s_lp, s_le = sem("lam_sums"), sem("lam_exps")
        s_nm, s_exp, s_es, s_comb = sem("nmax_ready"), sem("exp_done"), sem("sink_exp"), sem("probs_ready")
        s_pv = sem("pv_done")
        s_sso, s_so, s_o = sem("o_squares"), sem("o_std"), sem("o_ready")
        s_x1, s_h2 = sem("x1_ready"), sem("h2_ready")
        s_qTu, s_scu = sem("qT_used"), sem("scores_used")
        s_gd, s_ge, s_idx = sem("gate_shifted"), sem("gate_exp"), sem("experts_ready")
        s_got = [sem(f"row_got{j}") for j in range(2 * RING)]
        s_stg, s_clear = sem("staged"), sem("slots_cleared")
        s_dot, s_dgelu, s_wgt, s_acc = sem("row_dots"), sem("row_gelus"), sem("row_weights"), sem("row_sums")
        s_hhi, s_hlo = sem("h_hi_ready"), sem("h_lo_ready")
        s_u, s_v = [sem("u_loaded0"), sem("u_loaded1")], [sem("v_loaded0"), sem("v_loaded1")]
        s_uhi, s_ulo, s_vhi, s_vlo = sem("u_hi_ready"), sem("u_lo_ready"), sem("v_hi_ready"), sem("v_lo_ready")
        s_a, s_gelu, s_pw, s_whi, s_w = sem("a_done"), sem("gelu_done"), sem("w_product"), sem("w_hi"), sem("w_ready")
        s_yv = sem("v_product_done")
        s_g = [sem("gates_loaded0"), sem("gates_loaded1")]
        s_hot, s_gm, s_gt = sem("hot_rows_ready"), sem("gates_made"), sem("gates_taken")
        s_as, s_al = [sem("gelus_stored0"), sem("gelus_stored1")], [sem("gelus_loaded0"), sem("gelus_loaded1")]
        s_gst = [sem("gates_stored0"), sem("gates_stored1")]
        s_x2, s_f2, s_fm, s_fs, s_res = (sem(n) for n in ("x2_ready", "x2_squares", "x2_mean", "x2_std", "result_ready"))

        gates = nc.dram_tensor("gates", [DT // GB, P, NCHUNK, GB], f32).ap()
        spill = nc.dram_tensor("spill", [SPILL, P, DT], f32).ap()
        y_bank = [[bank["S0"], bank["S1"]], [bank["S2"], bank["T0"]], [bank["T1"], bank["G"]]]

        def after(eng, s, n):
            if isinstance(n, int) and n < 1:
                return
            eng.wait_ge(s, n)

        def within(i, last=NCHUNK - 1):
            return not isinstance(i, int) or i <= last

        def chunk_loop(eng, body, turns=((0, 1), (1, 9), (9, 10), (10, 11), (11, 12), (12, 15), (15, 16))):
            for first, end in turns:
                late = first * AHEAD >= MAIN
                if end - first == 1:
                    for c in range(AHEAD):
                        body(first * AHEAD + c, c, late, rows_of(first, c))
                else:
                    with eng.Fori(first, end) as t:
                        for c in range(AHEAD):
                            body(t * AHEAD + c, c, late, [] if late else rows_of(t, c))

        def place_of(n, g):
            return n % RING if isinstance(n, int) else g % RING

        def rows_of(t, c):
            first = (NCHUNK - EARLY) // AHEAD
            if not isinstance(t, int) or t < first:
                return [(12 * t + g, g) for g in range(12 * c // AHEAD, 12 * (c + 1) // AHEAD)]
            if t < first + 2:
                return [(12 * first + 4 * (t - first) + g, g) for g in range(4 * c // AHEAD, 4 * (c + 1) // AHEAD)]
            return []

        def chunk_of(m, late):
            if isinstance(m, int):
                late = m >= MAIN
            return m - MAIN if late else m + SPILL

        def over(i, c, n):
            return i // n if isinstance(i, int) else (i - c) // n + c // n

        BEFORE = [[(0, 1), (1, 4), (4, 5)], [(6, 7)], [(8, 10), (10, 11)]]

        def chunks_before(eng, turns, body):
            for first, end in turns:
                if end - first == 1:
                    for c in range(4):
                        body(4 * first + c, c)
                else:
                    with eng.Fori(first, end) as t:
                        for c in range(4):
                            body(t * 4 + c, c)

        def gate_blocks(eng, tile, body):
            if tile == 0:
                for b in range(4):
                    body(b, b % 2, 20 + b, 4 + b)
            else:
                with eng.Fori(2 * tile, 2 * tile + 2) as two:
                    for b in range(2):
                        body(2 * two + b, b, 2 * two + (12 + 12 * tile + b), 2 * two + (4 - 4 * tile + b))

        tally = {}

        def done(eng, ins, s):
            tally[s.name] = tally.get(s.name, 0) + 1
            ins.then_inc(s, 1)
            eng.wait_ge(s, tally[s.name])

        plan = head_plan()
        JOBS = [(i, j) for i in range(NT) for j in range(NHEADS)]
        first_map = []
        for i, j in JOBS:
            first_map.append(i * MAPS + sum(len(plan[a][1]) for a in range(j)))
        ADA_ORDER = [1, 0, 2, 4, 3, 5]
        ADA_HALVES = [(s, b) for s in ADA_ORDER for b in range(2)]

        N = len(JOBS)

        def key_tiles(i, j):
            return range(max(0, i - 1), i + 1) if plan[j][0] == "C" else range(i + 1)

        block = ctx.enter_context(nc.Block())

        @block.tensor
        def _(pe):
            def take(b, key):
                if fillings[b]:
                    pe.wait_ge(free[b], fillings[b])
                fillings[b] += 1
                turn[key] = (b, fillings[b])
                return bank[b]

            def emptied(key):
                b, n = turn[key]
                pe.wait_ge(free[b], n)

            pe.wait_ge(s_const, 6)
            mcols = take("G", "mod_cols")
            for n in range(4):
                pe.wait_ge(s_accd, n + 1)
                for m in range(4):
                    at = n * 4 + m
                    pe.matmul(mcols[:, at:at + 1], mod_acc[:, n % 2, m * P:m * P + P], ones[:, 0:1],
                              start=True, stop=False)
                    mm = pe.matmul(mcols[:, at:at + 1], b_half[0:1, n % 2, m * P:m * P + P], ones[0:1, 0:1],
                                   start=False, stop=True)
                mm.then_inc(full["G"] if n == 3 else s_modu, 1)
            for k in range(KD):
                b = f"T{k % 2}"
                ps = take(b, ("xT", k))
                for i in range(NT):
                    if k == 0:
                        pe.wait_ge(s_xn, i + 1)
                    mm = pe.transpose(ps[:, i * P:i * P + P], xn[:, i, k * P:k * P + P], ident[:, :])
                mm.then_inc(full[b], 1)

            def mod_row(n):
                ps = take("G", ("row", n))
                pe.wait_ge(s_accd, n + 1)
                pe.matmul(ps[:, :], ones[:, :], mod_acc[:, n % 2, :], start=True, stop=False)
                pe.matmul(ps[:, :], ones[0:1, :], b_half[0:1, n % 2, :], start=False, stop=True)\
                    .then_inc(full["G"], 1)

            for e in range(QK_TILES):
                b = f"S{e % 3}"
                ps = take(b, ("qk", e))
                pe.wait_ge(s_win[e % 4], 16 * (e // 4 + 1))
                for k in range(KD):
                    if e == 0:
                        emptied(("xT", k))
                    pe.matmul(ps[:, 0:GT * P], ring_w[:, e % 4, k * P:k * P + P], hT[:, k, 0:GT * P],
                              start=(k == 0), stop=(k == KD - 1))
                pe.wait_ge(s_inhi, e + 1)
                pe.wait_ge(s_inlo, e + 1)
                for k in range(KD):
                    if e == 0:
                        pe.wait_ge(s_h1hi, k + 1)
                        pe.wait_ge(s_h1lo, k + 1)
                    kk = slice(k * P, k * P + P)
                    pe.matmul(ps[:, GT * P:S], win_hi[:, e % 2, kk], h1_hi[:, k, :], start=(k == 0), stop=False)
                    pe.matmul(ps[:, GT * P:S], win_hi[:, e % 2, kk], h1_lo[k][:, :], start=False, stop=False)
                    mm = pe.matmul(ps[:, GT * P:S], win_lo[:, e % 2, kk], h1_hi[:, k, :],
                                   start=False, stop=(k == KD - 1))
                mm.then_inc(full[b], 1)
                if 2 <= e < 10:
                    mod_row(e + 2)
            for n in range(V_COLS // 256):
                e = QK_TILES + 2 * n
                for a in (e, e + 1):
                    pe.wait_ge(s_win[a % 4], 16 * (a // 4 + 1))
                w = ring_w[:, e % 4:e % 4 + 2, :].rearrange("p a (k c) -> p a k c", k=KD)
                for i in range(NT):
                    b = f"O{i % 2}"
                    ps = take(b, ("v", n, i))
                    for k in range(KD):
                        mm = pe.matmul(ps[:, 0:256], hT[:, k, i * P:i * P + P], w[:, :, k, :],
                                       start=(k == 0), stop=(k == KD - 1))
                    mm.then_inc(full[b], 1)

            for e in range(QK_TILES - 3, QK_TILES):
                emptied(("qk", e))
            maps_done = [0]

            def scores(J):
                i, j = JOBS[J]
                kt = key_tiles(i, j)
                for m, (qt, kk, part, rows) in enumerate(plan[j][1]):
                    b = f"S{maps_done[0] % 3}"
                    maps_done[0] += 1
                    ps = take(b, ("s", first_map[J] + m))
                    pe.matmul(ps[:, 0:len(kt) * P], qkT[part:part + rows, qt, i * P:i * P + P],
                              qkT[part:part + rows, kk, kt[0] * P:(kt[-1] + 1) * P],
                              start=True, stop=True).then_inc(full[b], 1)

            def transpose_probs(J):
                i, j = JOBS[J]
                b = f"T{J % 2}"
                ps = take(b, ("pT", J))
                if plan[j][0] == "A":
                    pe.wait_ge(s_comb, i * NA + plan[j][5] + 1)
                else:
                    pe.wait_ge(s_exp, first_map[J] + 1)
                for n, kt in enumerate(key_tiles(i, j)):
                    mm = pe.transpose(ps[:, n * P:n * P + P], Sb[:, first_map[J] % 8, n * P:n * P + P], ident[:, :])
                mm.then_inc(full[b], 1)

            def pv(J):
                i, j = JOBS[J]
                b = f"O{j // 8}"
                ps = take(b, ("o", i, j // 8)) if j % 8 == 0 else bank[b]
                if J == 0:
                    emptied(("v", 2, 2))
                    emptied(("v", 2, 3))
                emptied(("pT", J))
                col = plan[j][4]
                kt = key_tiles(i, j)
                for n, t in enumerate(kt):
                    mm = pe.matmul(ps[:, (j % 8) * HD:(j % 8) * HD + HD], pT[:, J % 2, n * P:n * P + P],
                                   v_sb[:, t, col:col + HD], start=(n == 0), stop=(n == len(kt) - 1))
                mm.then_inc(full[b] if j % 8 == 7 else s_pv, 1)

            def out_proj(i):
                for half in range(2):
                    b = f"T{half}"
                    ps = take(b, ("oT", i, half))
                    pe.wait_ge(s_o, i + 1)
                    for n in range(4):
                        k = half * 4 + n
                        mm = pe.transpose(ps[:, n * P:n * P + P], o_sb[:, k * P:k * P + P], ident[:, :])
                    mm.then_inc(full[b], 1)
                if i == 0:
                    pe.wait_ge(s_wout, 16)
                emptied(("oT", i, 0))
                emptied(("oT", i, 1))
                for half, b in enumerate(("G", "T0")):
                    ps = take(b, ("y", i, half))
                    for k in range(KD):
                        mm = pe.matmul(ps[:, :], oT[k // 4][:, k % 4, :],
                                       w_outs[:, k, half * 512:half * 512 + 512],
                                       start=(k == 0), stop=(k == KD - 1))
                    mm.then_inc(full[b], 1)

            scores(0)
            for J in range(N + 6):
                if J + 1 < N:
                    scores(J + 1)
                if 2 <= J < N + 2:
                    transpose_probs(J - 2)
                if 3 <= J < N + 3:
                    pv(J - 3)
                if J >= 6 and (J - 6) % NHEADS == NHEADS - 1:
                    out_proj((J - 6) // NHEADS)

            pe.wait_ge(s_h2, NT)
            for k in range(KD):
                b = f"T{k % 2}"
                ps = take(b, ("h2T", k))
                for i in range(NT):
                    mm = pe.transpose(ps[:, i * P:i * P + P], h2[:, i, k * P:k * P + P], ident[:, :])
                mm.then_inc(full[b], 1)
            kb = ["T0", "T1", "O0", "O1"]

            def key_scores(e):
                emptied(("q", e))
                for i in range(NT):
                    ps = take(kb[i], ("sc", e // 4, i)) if e % 4 == 0 else bank[kb[i]]
                    mm = pe.matmul(ps[:, (e % 4) * P:(e % 4) * P + P], qT[:, e % 3, i * P:i * P + P], keys[:, e, :],
                                   start=True, stop=True)
                    if e % 4 == 3:
                        mm.then_inc(full[kb[i]], 1)
                if e % 4 != 3:
                    mm.then_inc(s_qTu, 1)

            for e in range(2 * PH):
                b = f"S{e % 3}"
                ps = take(b, ("q", e))
                pe.wait_ge(s_wq[e % 4], 16 * (e // 4 + 1))
                for k in range(KD):
                    if e == 0:
                        emptied(("h2T", k))
                    pe.matmul(ps[:, 0:GT * P], ring_a[:, e % 4, k * P:k * P + P], hT[:, k, 0:GT * P],
                              start=(k == 0), stop=(k == KD - 1))
                pe.wait_ge(s_qhi, e + 1)
                pe.wait_ge(s_qlo, e + 1)
                for k in range(KD):
                    if e == 0:
                        pe.wait_ge(s_hhi, k + 1)
                        pe.wait_ge(s_hlo, k + 1)
                    kk = slice(k * P, k * P + P)
                    pe.matmul(ps[:, GT * P:S], wq_hi[:, e % 2, kk], h_hi[:, k, :], start=(k == 0), stop=False)
                    pe.matmul(ps[:, GT * P:S], wq_hi[:, e % 2, kk], h_lo[:, k, :], start=False, stop=False)
                    mm = pe.matmul(ps[:, GT * P:S], wq_lo[:, e % 2, kk], h_hi[:, k, :],
                                   start=False, stop=(k == KD - 1))
                mm.then_inc(full[b], 1)
                if e == 0:
                    pe.wait_ge(s_keys, 16)
                if e >= 1:
                    key_scores(e - 1)
            key_scores(2 * PH - 1)

            def a_chunk(i, c, part=range(KD)):
                if not within(i):
                    return
                ps = bank[f"O{c % 2}"]
                if part[0] == 0:
                    after(pe, s_gelu, i - 1)
                    pe.wait_ge(s_uhi, i + 1)
                    pe.wait_ge(s_ulo, i + 1)
                q = c % 2
                for k in part:
                    kk = slice(k * P, k * P + P)
                    pe.matmul(ps[:, 0:DT], u_hi[:, q, kk], h_hi[:, k, :], start=(k == 0), stop=False)
                    pe.matmul(ps[:, 0:DT], u_hi[:, q, kk], h_lo[:, k, :], start=False, stop=False)
                    mm = pe.matmul(ps[:, 0:DT], u_lo[:, q, kk], h_hi[:, k, :], start=False, stop=(k == KD - 1))
                if part[-1] == KD - 1:
                    mm.then_inc(s_a, 1)

            for i in range(NT):
                b, n = turn[("sc", 3, i)]
                pe.wait_ge(free[b], n)
            for k in range(KD):
                pe.wait_ge(s_hlo, k + 1)
                pe.wait_ge(s_hhi, k + 1)

            for tile in range(NT - GT):
                chunks_before(pe, BEFORE[tile], a_chunk)
                ps = take("G", ("cols", tile))
                pe.wait_ge(s_idx, tile + 1)
                for n, m in enumerate((key_f[:, tile + GT, 0, :], key_f[:, tile + GT, 1, :], gate[:, tile + GT, :])):
                    mm = pe.transpose(ps[:, n * P:n * P + P], m, ident[:, :])
                mm.then_inc(full["G"], 1)

                def block_gates(tb, parity, i, slot):
                    for b in range(GB // 4):
                        B = tb * (GB // 4) + b
                        ps = bank[f"T{b % 2}"]
                        after(pe, s_gt, B - 1)
                        pe.wait_ge(s_hot, B + 1)
                        for tok in range(4):
                            mm = pe.matmul(ps[:, tok * P:tok * P + P], hot_j[:, b % 2, tok, :], hot_i[:, b % 2, tok, :],
                                           start=True, stop=True)
                        mm.then_inc(s_gm, 1)
                        a_chunk(i, parity, range(b, b + 1))

                gate_blocks(pe, tile, block_gates)
            emptied(("cols", NT - GT - 1))
            pe.wait_ge(s_gt, DT // 4)

            def v_chunk(i, c):
                pe.wait_ge(s_w, i + 1)
                pe.wait_ge(s_vlo, i + 1)
                q = c % 2
                first, last = isinstance(i, int) and i == 0, isinstance(i, int) and i == NCHUNK - 1
                for t in range(NT - GT):
                    tt = slice(t * P, t * P + P)
                    for n, (w, v) in enumerate(((w_hi, v_hi), (w_hi, v_lo), (w_lo, v_hi))):
                        for half in range(2):
                            mm = pe.matmul(y_bank[t][half][:, :], w[:, q, tt], v[:, q, half * 512:half * 512 + 512],
                                           start=(first and n == 0), stop=(last and n == 2))
                mm.then_inc(s_yv, 1)

            def both(m, c, late, _):
                v_chunk(m, c)
                if not late and not (isinstance(m, int) and m + EARLY >= NCHUNK):
                    a_chunk(m + EARLY, c)

            chunk_loop(pe, both, ((0, 1), (1, 10), (10, 11), (11, 15), (15, 16)))

        def taken(eng, key):
            b, n = turn[key]
            eng.wait_ge(full[b], n)
            return bank[b]

        def emptied(eng, key):
            b, n = turn[key]
            eng.wait_ge(free[b], n)

        def half_used(eng, n):
            if n < 3:
                eng.wait_ge(s_modu, n + 1)
            else:
                taken(eng, "mod_cols" if n == 3 else ("row", n))

        def freeing(key):
            return free[turn[key][0]]

        def pv_done(eng, J):
            i, j = JOBS[J]
            if j % 8 == 7:
                taken(eng, ("o", i, j // 8))
            else:
                eng.wait_ge(s_pv, J + 1 - (J + 1) // 8)

        def map_bufs_free(eng, m):
            if m >= 8:
                J = max(a for a in range(N) if first_map[a] <= m - 8)
                taken(eng, ("pT", J))

        @block.sync
        def _(sp):
            def ada(n):
                s, b = ADA_HALVES[n]
                if n >= 2:
                    sp.wait_ge(s_accd, n - 1)
                    half_used(sp, n - 2)
                dst = ring_a[:, 4 * (n % 2):4 * (n % 2) + 4, :].rearrange("p a b -> p (a b)")
                at = s * D + b * 512
                sp.dma_start(dst.rearrange("p (k c) -> p k c", k=KD),
                             w_ada[:, at:at + 512].rearrange("(k p) c -> p k c", p=P)).then_inc(s_ada[n % 2], 16)
                sp.dma_start(b_half[0:1, n % 2, :], b_ada[0:1, at:at + 512]).then_inc(s_ada[n % 2], 16)

            def win(e):
                last = e - 4
                if last >= QK_TILES:
                    for i in (2, 3):
                        b, n = turn[("v", (last - QK_TILES) // 2, i)]
                        sp.wait_ge(full[b], n)
                elif last >= 0:
                    b, n = turn[("qk", last)]
                    sp.wait_ge(full[b], n)
                sp.dma_start(ring_w[:, e % 4, :], w_in[e]).then_inc(s_win[e % 4], 16)

            sp.dma_start(x_sb[:, :, :], x[0].rearrange("(t p) d -> p t d", p=P)).then_inc(s_x, 16)
            for n in range(4):
                ada(n)
            for e in range(4):
                win(e)
            ada(4)
            ada(5)
            for e in range(4, IN_TILES):
                win(e)
                if e + 2 < 12:
                    ada(e + 2)
            for i in (2, 3):
                b, n = turn[("v", 2, i)]
                sp.wait_ge(full[b], n)
            sp.dma_start(w_outs[:, :, :], w_out.rearrange("(k p) d -> p k d", p=P)).then_inc(s_wout, 16)
            sp.dma_start(keys[:, :, :], keys_t).then_inc(s_keys, 16)
            sp.wait_ge(s_accd, 12)
            for e in range(2 * PH):
                if e >= 4:
                    b, n = turn[("q", e - 4)]
                    sp.wait_ge(full[b], n)
                sp.dma_start(ring_a[:, e % 4, :], wq[e]).then_inc(s_wq[e % 4], 16)

            def load_u(i, c):
                if within(i):
                    after(sp, s_ulo, i - 1)
                    sp.dma_start(u_raw[:, c % 2, :], u_t[bass.ds(i, 1)].rearrange("o p d -> p (o d)"))\
                      .then_inc(s_u[c % 2], 16)

            def load_v(m, c, late):
                if within(m):
                    after(sp, s_vlo, m - 1)
                    sp.dma_start(v_raw[:, c % 2, :], peer_v[bass.ds(chunk_of(m, late) * P, P), :])\
                      .then_inc(s_v[c % 2], 16)

            def load_g(q, parity, late):
                if within(q, NCHUNK // 4 - 1):
                    after(sp, s_pw, 4 * (q - 1))
                    sp.dma_start(g_in[:, parity, :, :, :].rearrange("p b i t -> p b (i t)"),
                                 gates[:, :, bass.ds(chunk_of(4 * q, late), 4), :].rearrange("b p i t -> p b (i t)"))\
                      .then_inc(s_g[parity], 16)
                    if late or (isinstance(q, int) and 4 * q >= MAIN):
                        sp.dma_start(a_act[:, 4 * parity:4 * parity + 4, :],
                                     spill[bass.ds(q * 4 - MAIN, 4)].rearrange("i p t -> p i t"))\
                          .then_inc(s_al[parity], 16)

            for e in (13, 14, 15):
                b, n = turn[("q", e)]
                sp.wait_ge(full[b], n)
            load_u(0, 0)
            load_u(1, 1)
            with sp.Fori(1, EARLY // 2 + 1) as two:
                load_u(2 * two, 0)
                load_u(2 * two + 1, 1)
            for parity in range(2):
                sp.wait_ge(s_gst[parity], 16 * (DT // GB // 2))
            sp.wait_ge(s_idx, NT)
            for q in range(2):
                load_g(q, q, False)
                load_v(q, q, False)

            def loads(m, c, late, _):
                if isinstance(m, int) and m == MAIN:
                    sp.wait_ge(s_ulo, NCHUNK)
                    sp.dma_start(fin_row[:, :], final_row.partition_broadcast(P)).then_inc(s_fin, 16)
                load_v(m + 2, c, late)
                if not late:
                    load_u(m + EARLY + 2, c)
                if c % 4 == 3:
                    load_g(over(m, c, 4) + 2, c // 4, late)

            chunk_loop(sp, loads)
            for i in range(NT):
                sp.wait_ge(s_res, i + 1)
                sp.dma_start(out[0, i * P:i * P + P, :], x_sb[:, i, :]).then_inc(s_out, 16)
            sp.wait_ge(s_out, 16 * NT)

        @block.gpsimd
        def _(pool):
            pool.memset(ident[:, :], 0.0).then_inc(s_const, 1)
            pool.memset(ones[:, :], 1.0).then_inc(s_const, 1)
            pool.iota(ndist[:, :], [[1, S]], base=-(S - P), channel_multiplier=-1,
                      allow_small_or_imprecise_dtypes=True).then_inc(s_const, 1)
            pool.iota(iota16[:, :], [[1, TOPK]], base=0, channel_multiplier=0,
                      allow_small_or_imprecise_dtypes=True).then_inc(s_const, 1)
            pool.iota(iota_k[:, :], [[1, NKEYS]], base=0, channel_multiplier=0,
                      allow_small_or_imprecise_dtypes=True).then_inc(s_const, 1)
            pool.wait_ge(s_const, 5)
            pool.affine_select(out=ident[:, :], in_=ident[:, :], compare_op=ALU.not_equal, fill=1.0, base=0,
                               pattern=[[-1, P]], channel_multiplier=1).then_inc(s_const, 1)
            pool.affine_select(out=ndist[:, :], in_=ndist[:, :], compare_op=ALU.is_ge, fill=MASKED, base=S - P,
                               pattern=[[-1, S]], channel_multiplier=1).then_inc(s_const, 1)
            pool.wait_ge(s_const, 7)
            pool.affine_select(out=ndist_w[:, :], in_=ndist[:, 2 * P:4 * P], compare_op=ALU.is_ge, fill=MASKED,
                               base=-1, pattern=[[1, 2 * P]], channel_multiplier=-1).then_inc(s_const, 1)

            def win_low(e):
                pool.wait_ge(s_inhi, e + 1)
                if e >= 2:
                    b, n = turn[("qk", e - 2)]
                    pool.wait_ge(full[b], n)
                pool.tensor_tensor(win_lo[:, e % 2, :], ring_w[:, e % 4, :], win_hi[:, e % 2, :].bitcast(f32),
                                   ALU.subtract).then_inc(s_inlo, 1)

            win_low(0)
            win_low(1)
            for k in range(KD):
                emptied(pool, ("xT", k))
                pool.wait_ge(s_h1hi, k + 1)
                pool.tensor_tensor(h1_lo[k][:, :], hT[:, k, GT * P:S], h1_hi[:, k, :].bitcast(f32), ALU.subtract)\
                    .then_inc(s_h1lo, 1)
            for e in range(2, QK_TILES):
                win_low(e)

            def wq_low(e):
                pool.wait_ge(s_qhi, e + 1)
                if e >= 2:
                    b, n = turn[("q", e - 2)]
                    pool.wait_ge(full[b], n)
                pool.tensor_tensor(wq_lo[:, e % 2, :], ring_a[:, e % 4, :], wq_hi[:, e % 2, :].bitcast(f32),
                                   ALU.subtract).then_inc(s_qlo, 1)

            for k in range(KD):
                emptied(pool, ("h2T", k))
                pool.wait_ge(s_hhi, k + 1)
                pool.tensor_tensor(h_lo[:, k, :], hT[:, k, GT * P:S], h_hi[:, k, :].bitcast(f32), ALU.subtract)\
                    .then_inc(s_hlo, 1)
                if k in (1, 3):
                    wq_low(k // 2)
            for e in range(2, 2 * PH):
                wq_low(e)

            def split_u(i, c):
                if not within(i):
                    return
                pool.wait_ge(s_uhi, i + 1)
                pool.tensor_tensor(u_lo[:, c % 2, :], u_raw[:, c % 2, :], u_hi[:, c % 2, :].bitcast(f32),
                                   ALU.subtract).then_inc(s_ulo, 1)

            split_u(0, 0)
            for tile in range(NT - GT):
                chunks_before(pool, BEFORE[tile], lambda i, c: split_u(i + 1, c + 1))
                gate_blocks(pool, tile, lambda tb, parity, i, slot: split_u(i + 1, parity + 1))

            def gather(n, c):
                if not within(n):
                    return
                place = place_of(n, c)
                if not isinstance(n, int) or n >= RING:
                    pool.wait_ge(s_dot, n + 1 - RING)
                    pool.sem_inc(s_clear, 1)
                    pool.wait_ge(s_acc, n + 1 - RING)
                    pool.sem_inc(s_clear, 1)
                pool.tensor_copy(stage[:, place:place + 1], eidx[:, bass.ds(n, 1)]).then_inc(s_stg, 1)
                pool.wait_ge(s_stg, n + 1)
                pool.sem_inc(s_clear, 1)
                for table, slot in ((peer_u, 2 * place), (peer_v, 2 * place + 1)):
                    pool.indirect_dma_start(rows[slot][:, :], None, table[:, :],
                                            bass.IndirectOffsetOnAxis(stage[:, place:place + 1], 0))\
                        .then_inc(s_got[slot], 16)

            pool.wait_ge(s_idx, NT)
            for parity in range(2):
                pool.wait_ge(s_gst[parity], 16 * (DT // GB // 2))
            for n in range(RING - 2):
                gather(n, n)

            def split_and_gather(m, c, late, numbers):
                for n, g in numbers:
                    gather(n + RING - 2, g + RING - 2)
                if not late:
                    split_u(m + EARLY + 1, c + 1)

            chunk_loop(pool, split_and_gather)

        @block.scalar
        def _(act):
            act.dma_start(c_in[:, :], c_col).then_inc(s_c, 16)
            act.dma_start(n1_col[:, :], norm1_col).then_inc(s_n1, 16)
            act.dma_start(lam_in[:, :, :].rearrange("p a b -> p (a b)"), lam_vecs.partition_broadcast(P))\
               .then_inc(s_lam, 16)
            act.dma_start(subln[:, :], subln_row.partition_broadcast(P)).then_inc(s_small, 16)
            act.dma_start(sinks[:, :], sinks_row.partition_broadcast(P)).then_inc(s_small, 16)
            act.dma_start(a2_row[:, :], norm2_row.partition_broadcast(P)).then_inc(s_small, 16)
            act.wait_ge(s_c, 16)
            act.activation(c_tmp[:, :], c_in[:, :], ACT.Exp, scale=-1.0).then_inc(s_ce, 1)
            act.wait_ge(s_lp, 1)
            act.activation(lam_s[:, 2:4], lam_s[:, 0:2], ACT.Exp).then_inc(s_le, 1)
            act.wait_ge(s_x, 16)
            for i in range(NT):
                act.activation(xn[:, i, :], x_sb[:, i, :], ACT.Square, accum_out=ss[:, i:i + 1]).then_inc(s_ss, 1)
            act.wait_ge(s_ms, 1)
            act.activation(rstd[:, 0:NT], ss[:, 0:NT], ACT.Sqrt).then_inc(s_std, 1)

            def win_high(e):
                if e >= 2:
                    taken(act, ("qk", e - 2))
                act.wait_ge(s_win[e % 4], 16 * (e // 4 + 1))
                act.activation(win_hi[:, e % 2, :], ring_w[:, e % 4, :], ACT.Copy).then_inc(s_inhi, 1)

            win_high(0)
            win_high(1)
            emptied(act, "mod_cols")
            for k in range(KD):
                ps = taken(act, ("xT", k))
                act.activation(hT[:, k, :], ps[:, :], ACT.Identity, scale=a1_col[:, k:k + 1],
                               bias=sh1_col[:, k:k + 1]).then_inc(freeing(("xT", k)), 1)
                emptied(act, ("xT", k))
                act.activation(h1_hi[:, k, :], hT[:, k, GT * P:S], ACT.Copy).then_inc(s_h1hi, 1)
            for e in range(QK_TILES):
                ps = taken(act, ("qk", e))
                act.activation(qkT[:, e, :], ps[:, :], ACT.Copy).then_inc(freeing(("qk", e)), 1)
                if e + 2 < QK_TILES:
                    win_high(e + 2)

            def exps(J):
                i, j = JOBS[J]
                kind, maps, scale, _, _, c, _ = plan[j]
                n = len(key_tiles(i, j)) * P
                for m in range(first_map[J], first_map[J] + len(maps)):
                    act.wait_ge(s_nm, m + 1)
                    act.activation(Sb[:, m % 8, 0:n], Sb[:, m % 8, 0:n], ACT.Exp, scale=scale,
                                   bias=nmax[:, m:m + 1], accum_out=den[:, m:m + 1]).then_inc(s_exp, 1)
                if kind == "C":
                    a = i * NCH + c
                    act.activation(esink[:, a:a + 1], sinks[:, c:c + 1], ACT.Exp,
                                   bias=nmax[:, m:m + 1]).then_inc(s_es, 1)

            def take_pT(J):
                n = len(key_tiles(*JOBS[J])) * P
                ps = taken(act, ("pT", J))
                if J >= 2:
                    pv_done(act, J - 2)
                act.activation(pT[:, J % 2, 0:n], ps[:, 0:n], ACT.Copy).then_inc(freeing(("pT", J)), 1)

            act.wait_ge(s_accd, 12)
            for J in range(N + 7):
                if J < N:
                    exps(J)
                if 2 <= J < N + 2:
                    take_pT(J - 2)
                if J >= 3 and (J - 3) % NHEADS == NHEADS - 1:
                    i = (J - 3) // NHEADS
                    act.wait_ge(s_sso, i + 1)
                    act.activation(sso[:, i, :, 1], sso[:, i, :, 0], ACT.Sqrt).then_inc(s_so, 1)
                if J >= 7 and (J - 7) % NHEADS == NHEADS - 1:
                    i = (J - 7) // NHEADS
                    act.wait_ge(s_ms, 2 + i)
                    act.activation(rstd[:, NT + i:NT + i + 1], ss[:, NT + i:NT + i + 1], ACT.Sqrt).then_inc(s_std, 1)
                if J >= 6 and (J - 6) % NHEADS == NHEADS - 1:
                    i = (J - 6) // NHEADS
                    for half in range(2):
                        ps = taken(act, ("oT", i, half))
                        if i >= 1 and half == 0:
                            taken(act, ("y", i - 1, 1))
                        act.activation(oT[half][:, :, :], ps[:, :].rearrange("p (a b) -> p a b", b=P),
                                       ACT.Copy).then_inc(freeing(("oT", i, half)), 1)

            def wq_high(e):
                if e >= 2:
                    taken(act, ("q", e - 2))
                act.wait_ge(s_wq[e % 4], 16 * (e // 4 + 1))
                act.activation(wq_hi[:, e % 2, :], ring_a[:, e % 4, :], ACT.Copy).then_inc(s_qhi, 1)

            wq_high(0)
            wq_high(1)
            for k in range(KD):
                ps = taken(act, ("h2T", k))
                act.activation(hT[:, k, :], ps[:, :], ACT.Copy).then_inc(freeing(("h2T", k)), 1)
                taken(act, ("y", NT - 1, 1))
                emptied(act, ("h2T", k))
                act.activation(h_hi[:, k, :], hT[:, k, GT * P:S], ACT.Copy).then_inc(s_hhi, 1)

            def take_scores(g):
                for i in range(NT):
                    ps = taken(act, ("sc", g, i))
                    n = g * NT + i
                    if n >= 8:
                        act.wait_ge(s_scu, n - 7)
                    act.activation(sc[:, n % 8, :], ps[:, :], ACT.Copy).then_inc(freeing(("sc", g, i)), 1)

            for e in range(2 * PH):
                ps = taken(act, ("q", e))
                if e >= 3:
                    last = e - 3
                    if last % 4 == 3:
                        taken(act, ("sc", last // 4, NT - 1))
                    else:
                        act.wait_ge(s_qTu, last + 1 - (last + 1) // 4)
                act.activation(qT[:, e % 3, :], ps[:, :], ACT.Copy).then_inc(freeing(("q", e)), 1)
                if e + 2 < 2 * PH:
                    wq_high(e + 2)
                if e % 4 == 0 and e:
                    take_scores(e // 4 - 1)
            take_scores(3)

            def u_high(i, c):
                if not within(i):
                    return
                after(act, s_a, i - 1)
                act.wait_ge(s_u[c % 2], 16 * (over(i, c, 2) + 1))
                act.activation(u_hi[:, c % 2, :], u_raw[:, c % 2, :], ACT.Copy).then_inc(s_uhi, 1)

            def v_high(i, c):
                if not within(i):
                    return
                after(act, s_yv, i - 1)
                act.wait_ge(s_v[c % 2], 16 * (over(i, c, 2) + 1))
                act.activation(v_hi[:, c % 2, :], v_raw[:, c % 2, :], ACT.Copy).then_inc(s_vhi, 1)

            def gelu(i, slot, c):
                if not within(i):
                    return
                act.wait_ge(s_a, i + 1)
                act.activation(a_act[:, bass.ds(slot, 1), :].rearrange("p o t -> p (o t)"),
                               bank[f"O{c % 2}"][:, 0:DT], ACT.Gelu).then_inc(s_gelu, 1)

            def gelu_to_dram(i, slot, c):
                after(act, s_as[c % 2], 16 * over(i, c, 2))
                gelu(i, slot, c)
                act.wait_ge(s_gelu, i + 1)
                act.dma_start(spill[bass.ds(i, 1)].rearrange("o p t -> p (o t)"),
                              a_act[:, bass.ds(slot, 1), :].rearrange("p o t -> p (o t)")).then_inc(s_as[c % 2], 16)

            def early(i, c):
                u_high(i + 1, c + 1)
                if isinstance(i, int) and i >= SPILL:
                    act.wait_ge(s_as[c % 2], 16 * (SPILL // 2))
                    gelu(i, c, c)
                else:
                    gelu_to_dram(i, c, c)

            def exp_gates(n):
                tile = (n + GT) % NT
                act.wait_ge(s_gd, n + 1)
                act.activation(gate[:, tile, :], gate[:, tile, :], ACT.Exp).then_inc(s_ge, 1)

            u_high(0, 0)
            exps_at = {(0, 2): 0, (1, 0): 1, (2, 0): 2, (2, 1): 3}
            for tile in range(NT - GT):
                for n, turns in enumerate(BEFORE[tile]):
                    if (tile, n) in exps_at:
                        exp_gates(exps_at[tile, n])
                    chunks_before(act, [turns], early)

                def take_gates(tb, parity, i, slot):
                    u_high(i + 1, parity + 1)
                    after(act, s_gst[parity], 16 * over(tb, parity, 2))
                    for b in range(GB // 4):
                        B = tb * (GB // 4) + b
                        act.wait_ge(s_gm, B + 1)
                        act.activation(g_out[parity][:, :, 4 * b:4 * b + 4].rearrange("p i t -> p t i"),
                                       bank[f"T{b % 2}"][:, :].rearrange("p (t i) -> p t i", t=4), ACT.Copy)\
                           .then_inc(s_gt, 1)
                    act.wait_ge(s_gt, (tb + 1) * (GB // 4))
                    act.dma_start(gates[bass.ds(tb, 1)].rearrange("o p i t -> p (o i t)"),
                                  g_out[parity][:, :, :].rearrange("p i t -> p (i t)")).then_inc(s_gst[parity], 16)
                    if tile < 2:
                        gelu_to_dram(i, slot, parity)
                    else:
                        gelu(i, slot, parity)

                gate_blocks(act, tile, take_gates)
            for parity in range(2):
                act.wait_ge(s_gst[parity], 16 * (DT // GB // 2))
            v_high(0, 0)

            def parts(m, c, late, numbers):
                v_high(m + 1, c + 1)
                for n, g in numbers:
                    act.wait_ge(s_dot, n + 1)
                    after(act, s_wgt, n - 1)
                    act.activation(act_g[:, g % 2:g % 2 + 1], dots[:, g % 2:g % 2 + 1], ACT.Gelu).then_inc(s_dgelu, 1)
                if not late:
                    u_high(m + EARLY + 1, c + 1)
                    if within(m + EARLY):
                        act.wait_ge(s_pw, m + 1)
                    gelu(m + EARLY, c, c)

            def squares(i):
                act.activation(rows[0][:, :], x_sb[:, i, :], ACT.Square,
                               accum_out=ss[:, 2 * NT + i:2 * NT + i + 1]).then_inc(s_f2, 1)

            def std(n, lo, hi):
                act.wait_ge(s_fm, n + 1)
                act.activation(rstd[:, 2 * NT + lo:2 * NT + hi], ss[:, 2 * NT + lo:2 * NT + hi], ACT.Sqrt)\
                   .then_inc(s_fs, 1)

            def parts_and_tile(m, c, late, numbers):
                parts(m, c, late, numbers)
                if isinstance(m, int) and m == NCHUNK - AHEAD + 1:
                    act.wait_ge(s_x2, 1)
                    squares(0)
                if isinstance(m, int) and m == NCHUNK - AHEAD + 3:
                    std(0, 0, GT)

            chunk_loop(act, parts_and_tile)
            for i in range(GT, NT):
                act.wait_ge(s_x2, 1 + 2 * (i - GT + 1))
                act.wait_ge(s_f2, i)
                squares(i)
            std(1, GT, NT)

        @block.vector
        def _(dve):
            def bcast(ap, shape):
                return ap.to_broadcast(shape)

            dve.wait_ge(s_ce, 1)
            done(dve, dve.tensor_scalar(c_tmp[:, :], c_tmp[:, :], 1.0, None, ALU.add), s_dv)
            done(dve, dve.reciprocal(c_tmp[:, :], c_tmp[:, :]), s_dv)
            done(dve, dve.tensor_tensor(c_silu[:, :], c_in[:, :], c_tmp[:, :], ALU.mult), s_dv)
            dve.wait_ge(s_lam, 16)
            done(dve, dve.tensor_tensor(lam_prod[:, :, :], lam_in[:, 0:4:2, :], lam_in[:, 1:4:2, :], ALU.mult), s_dv)
            dve.tensor_reduce(lam_s[:, 0:2], lam_prod[:, :, :], AX, ALU.add).then_inc(s_lp, 1)
            dve.wait_ge(s_le, 1)
            done(dve, dve.tensor_tensor(lam_s[:, 4:5], lam_s[:, 3:4], lam_s[:, 2:3], ALU.subtract), s_dv)
            done(dve, dve.tensor_scalar(lam_s[:, 5:6], lam_s[:, 4:5], -LAM_INIT, None, ALU.add), s_dv)
            dve.wait_ge(s_small, 48)
            done(dve, dve.tensor_scalar(subln[:, :], subln[:, :], 1.0 - LAM_INIT, None, ALU.mult), s_dv)
            done(dve, dve.tensor_scalar(nsinks[:, :], sinks[:, :], -1.0, None, ALU.mult), s_dv)
            dve.wait_ge(s_ss, NT)
            dve.tensor_scalar(ss[:, 0:NT], ss[:, 0:NT], 1.0 / D, EPS, ALU.mult, ALU.add).then_inc(s_ms, 1)
            dve.wait_ge(s_std, 1)
            done(dve, dve.reciprocal(rstd[:, 0:NT], rstd[:, 0:NT]), s_dv)
            for i in range(NT):
                dve.tensor_scalar(xn[:, i, :], x_sb[:, i, :], rstd[:, i:i + 1], None, ALU.mult).then_inc(s_xn, 1)

            def mod_half(n):
                acc = mod_acc[:, n % 2, :]
                w = ring_a[:, 4 * (n % 2):4 * (n % 2) + 4, :].rearrange("p a b -> p (a b)")\
                    .rearrange("p (k c) -> p k c", k=KD)
                if n >= 2:
                    half_used(dve, n - 2)
                dve.wait_ge(s_ada[n % 2], 32 * (n // 2 + 1))
                done(dve, dve.tensor_scalar(acc, w[:, 0, :], c_silu[:, 0:1], None, ALU.mult), s_dv)
                for k in range(1, KD):
                    ins = dve.scalar_tensor_tensor(out=acc, in0=w[:, k, :], scalar=c_silu[:, k:k + 1], in1=acc,
                                                   op0=ALU.mult, op1=ALU.add)
                    if k < KD - 1:
                        done(dve, ins, s_dv)
                    else:
                        ins.then_inc(s_accd, 1)

            def mod_row(n):
                ps = taken(dve, ("row", n))
                dst = {2: g1_row, 4: a2_row, 3: sh2_row, 5: g2_row}[ADA_HALVES[n][0]]
                at = slice(512 * ADA_HALVES[n][1], 512 * ADA_HALVES[n][1] + 512)
                if ADA_HALVES[n][0] == 4:
                    ins = dve.scalar_tensor_tensor(out=dst[:, at], in0=ps[:, :], scalar=1.0, in1=dst[:, at],
                                                   op0=ALU.add, op1=ALU.mult)
                else:
                    ins = dve.tensor_copy(dst[:, at], ps[:, :])
                ins.then_inc(freeing(("row", n)), 1)

            for n in range(4):
                mod_half(n)
            mcols = taken(dve, "mod_cols")
            dve.wait_ge(s_n1, 16)
            done(dve, dve.scalar_tensor_tensor(out=a1_col[:, :], in0=mcols[:, 0:8], scalar=1.0, in1=n1_col[:, :],
                                               op0=ALU.add, op1=ALU.mult), s_dv)
            dve.tensor_copy(sh1_col[:, :], mcols[:, 8:16]).then_inc(freeing("mod_cols"), 1)
            mod_half(4)
            for n in range(5, 12):
                mod_half(n)
                mod_row(n - 1)
            mod_row(11)
            emptied(dve, ("row", 11))
            for n in range(V_COLS // 256):
                for i in range(NT):
                    ps = taken(dve, ("v", n, i))
                    dve.tensor_copy(v_sb[:, i, 256 * n:256 * n + 256], ps[:, 0:256]).then_inc(freeing(("v", n, i)), 1)

            dve.wait_ge(s_const, 8)

            def soft_in(J):
                i, j = JOBS[J]
                kind, maps, scale, slope, _, c, _ = plan[j]
                n = len(key_tiles(i, j)) * P
                nd = ndist_w[:, 2 * P - n:2 * P] if kind == "C" else ndist[:, S - n:S]
                for m in range(first_map[J], first_map[J] + len(maps)):
                    ps = taken(dve, ("s", m))
                    map_bufs_free(dve, m)
                    dve.scalar_tensor_tensor(out=Sb[:, m % 8, 0:n], in0=nd, scalar=slope / scale, in1=ps[:, 0:n],
                                             op0=ALU.mult, op1=ALU.add).then_inc(freeing(("s", m)), 1)
                    emptied(dve, ("s", m))
                    done(dve, dve.tensor_reduce(mx[:, m:m + 1], Sb[:, m % 8, 0:n], AX, ALU.max), s_dv)
                    if kind == "C":
                        dve.tensor_scalar(nmax[:, m:m + 1], mx[:, m:m + 1], -scale, nsinks[:, c:c + 1],
                                          ALU.mult, ALU.min).then_inc(s_nm, 1)
                    else:
                        dve.tensor_scalar(nmax[:, m:m + 1], mx[:, m:m + 1], -scale, None, ALU.mult).then_inc(s_nm, 1)

            def post(J):
                i, j = JOBS[J]
                kind, maps, _, _, _, c, _ = plan[j]
                m = first_map[J]
                dve.wait_ge(s_exp, m + len(maps))
                if kind == "A":
                    a = i * NA + c
                    r = ra[:, a, 0:1]
                    dve.reciprocal(rden[:, i, j:j + 1], den[:, m:m + 1]).then_inc(s_rden, 1)
                    done(dve, dve.reciprocal(r, den[:, m + 1:m + 2]), s_dv)
                    done(dve, dve.scalar_tensor_tensor(out=r, in0=den[:, m:m + 1], scalar=lam_s[:, 5:6], in1=r,
                                                       op0=ALU.mult, op1=ALU.mult), s_dv)
                    n = len(key_tiles(i, j)) * P
                    one, two = Sb[:, m % 8, 0:n], Sb[:, (m + 1) % 8, 0:n]
                    dve.scalar_tensor_tensor(out=one, in0=two, scalar=r, in1=one,
                                             op0=ALU.mult, op1=ALU.add).then_inc(s_comb, 1)
                    return
                if kind == "C":
                    a = i * NCH + c
                    dve.wait_ge(s_es, a + 1)
                    done(dve, dve.tensor_tensor(den[:, m:m + 1], den[:, m:m + 1], esink[:, a:a + 1], ALU.add), s_dv)
                dve.reciprocal(rden[:, i, j:j + 1], den[:, m:m + 1]).then_inc(s_rden, 1)

            def heads_out(i):
                taken(dve, ("o", i, 0))
                taken(dve, ("o", i, 1))
                if i:
                    taken(dve, ("oT", i - 1, 1))
                dve.wait_ge(s_rden, (i + 1) * NHEADS)
                for b in range(2):
                    dve.tensor_tensor(o_sb[:, b * 512:b * 512 + 512].rearrange("p (h d) -> p h d", d=HD),
                                      bank[f"O{b}"][:, :].rearrange("p (h d) -> p h d", d=HD),
                                      rden[:, i, 8 * b:8 * b + 8].unsqueeze(2).to_broadcast([P, 8, HD]),
                                      ALU.mult).then_inc(free[f"O{b}"], 1)
                for b in range(2):
                    emptied(dve, ("o", i, b))
                oa = o_sb[:, :].rearrange("p (g h d) -> p g h d", g=NA, d=HD)[:, :, 0, :]
                sq = rep[:, 0:NA * HD].rearrange("p (h d) -> p h d", d=HD)
                done(dve, dve.tensor_tensor(sq, oa, oa, ALU.mult), s_dv)
                done(dve, dve.tensor_reduce(sso[:, i, :, 0], sq, AX, ALU.add), s_dv)
                dve.tensor_scalar(sso[:, i, :, 0], sso[:, i, :, 0], 1.0 / HD, EPS, ALU.mult, ALU.add).then_inc(s_sso, 1)
                dve.wait_ge(s_so, i + 1)
                done(dve, dve.reciprocal(sso[:, i, :, 1], sso[:, i, :, 1]), s_dv)
                done(dve, dve.tensor_tensor(oa, oa, sso[:, i, :, 1].unsqueeze(2).to_broadcast([P, NA, HD]),
                                            ALU.mult), s_dv)
                dve.tensor_tensor(oa, oa, subln[:, :].unsqueeze(1).to_broadcast([P, NA, HD]), ALU.mult).then_inc(s_o, 1)

            flat = mod_acc[:, :, :].rearrange("p a b -> p (a b)")

            def second_norm(i):
                r = slice(NT + i, NT + i + 1)
                done(dve, dve.tensor_tensor_reduce(out=flat, in0=x_sb[:, i, :], in1=x_sb[:, i, :], scale=1.0,
                                                   scalar=0.0, op0=ALU.mult, op1=ALU.add, accum_out=ss[:, r]), s_dv)
                dve.tensor_scalar(ss[:, r], ss[:, r], 1.0 / D, EPS, ALU.mult, ALU.add).then_inc(s_ms, 1)
                dve.wait_ge(s_std, 2 + i)
                done(dve, dve.reciprocal(rstd[:, r], rstd[:, r]), s_dv)
                done(dve, dve.scalar_tensor_tensor(out=h2[:, i, :], in0=x_sb[:, i, :], scalar=rstd[:, r],
                                                   in1=a2_row[:, :], op0=ALU.mult, op1=ALU.mult), s_dv)
                dve.tensor_tensor(h2[:, i, :], h2[:, i, :], sh2_row[:, :], ALU.add).then_inc(s_h2, 1)

            def add_mixer(i):
                for half in range(2):
                    at = slice(512 * half, 512 * half + 512)
                    ps = taken(dve, ("y", i, half))
                    dve.tensor_tensor(mod_acc[:, half, :], ps[:, :], g1_row[:, at], ALU.mult)\
                       .then_inc(freeing(("y", i, half)), 1)
                    emptied(dve, ("y", i, half))
                    ins = dve.tensor_tensor(x_sb[:, i, at], x_sb[:, i, at], mod_acc[:, half, :], ALU.add)
                    done(dve, ins, s_x1 if half else s_dv)

            for J in range(N + 7):
                if J < N:
                    soft_in(J)
                if 1 <= J <= N:
                    post(J - 1)
                if J >= 3 and (J - 3) % NHEADS == NHEADS - 1:
                    heads_out((J - 3) // NHEADS)
                if J >= 7 and (J - 7) % NHEADS == NHEADS - 1:
                    add_mixer((J - 7) // NHEADS)
                    second_norm((J - 7) // NHEADS)

            dve.wait_ge(s_h2, NT)

            def best16(src, values, places, copy):
                step = s_dv
                for a, v in zip(src, values):
                    last = dve.max(v[:, 0:8], a)
                    if a is not src[-1]:
                        last.then_inc(step, 1)
                        tally[step.name] += 1
                done(dve, last, step)
                for a, v, q, t in zip(src, values, places, copy):
                    dve.max_index(q[:, 0:8], v[:, 0:8], a)
                    last = dve.match_replace(t, v[:, 0:8], a, -3.0e38)
                    if a is not src[-1]:
                        last.then_inc(step, 1)
                        tally[step.name] += 1
                done(dve, last, step)
                for t, v in zip(copy, values):
                    last = dve.max(v[:, 8:16], t)
                    if t is not copy[-1]:
                        last.then_inc(step, 1)
                        tally[step.name] += 1
                done(dve, last, step)
                for t, v, q in zip(copy, values, places):
                    last = dve.max_index(q[:, 8:16], v[:, 8:16], t)
                    if t is not copy[-1]:
                        last.then_inc(step, 1)
                        tally[step.name] += 1
                done(dve, last, step)

            for g in range(4):
                for i in range(NT):
                    n = g * NT + i
                    emptied(dve, ("sc", g, i))
                    heads = [(2 * g + a, s) for a in range(2) for s in range(2)]
                    best16([sc[:, n % 8, P * q:P * q + P] for q in range(4)],
                           [sv[:, i, h, s, :] for h, s in heads], [si[:, i, h, s, :] for h, s in heads],
                           [rep[:, P * q:P * q + P] for q in range(4)])
                    for a in range(2):
                        h = 2 * g + a
                        ins = dve.tensor_tensor(cand[:, a, :, :],
                                                sv[:, i, h, 0, :].unsqueeze(2).to_broadcast([P, TOPK, TOPK]),
                                                sv[:, i, h, 1, :].unsqueeze(1).to_broadcast([P, TOPK, TOPK]), ALU.add)
                        if a:
                            ins.then_inc(s_scu, 1)
                    dve.wait_ge(s_scu, n + 1)
                    best16([cand[:, a, :, :].rearrange("p a b -> p (a b)") for a in range(2)],
                           [topv[:, i, 2 * g + a, :] for a in range(2)], [topp[:, i, 2 * g + a, :] for a in range(2)],
                           [rep[:, 256 * a:256 * a + 256] for a in range(2)])

            HK = PH * TOPK

            def decode(i):
                gt = gate[:, i, :].rearrange("p (h k) -> p h k", k=TOPK)
                done(dve, dve.tensor_tensor(gt, topv[:, i, :, :], topv[:, i, :, 0:1].to_broadcast([P, PH, TOPK]),
                                            ALU.subtract), s_gd)
                pos = topp[:, i, :, :].rearrange("p h k -> p (h k)")
                done(dve, dve.tensor_scalar(side_u[:, 0, :], pos, 4, None, ALU.logical_shift_right), s_dv)
                done(dve, dve.tensor_scalar(side_u[:, 1, :], pos, 15, None, ALU.bitwise_and), s_dv)
                done(dve, dve.tensor_copy(side_f[:, :, :], side_u[:, :, :]), s_dv)
                done(dve, dve.tensor_copy(sif[:, :, :, :], si[:, i, :, :, :]), s_dv)
                for s in range(2):
                    hot = onehot.rearrange("p (a b) -> p a b", b=TOPK)
                    done(dve, dve.tensor_tensor(hot, iota16[:, :].unsqueeze(1).to_broadcast([P, HK, TOPK]),
                                                side_f[:, s, :].unsqueeze(2).to_broadcast([P, HK, TOPK]),
                                                ALU.is_equal), s_dv)
                    for h in range(PH):
                        hot = onehot.rearrange("p (h k a) -> p h k a", k=TOPK, a=TOPK)[:, h, :, :]
                        ins = dve.tensor_tensor(hot, hot, sif[:, h, s, :].unsqueeze(1).to_broadcast([P, TOPK, TOPK]),
                                                ALU.mult)
                        tally[s_dv.name] += 1
                        ins.then_inc(s_dv, 1)
                    dve.wait_ge(s_dv, tally[s_dv.name])
                    done(dve, dve.tensor_reduce(key_f[:, i, s, :], onehot.rearrange("p (a b) -> p a b", b=TOPK),
                                                AX, ALU.add), s_dv)
                if i < GT:
                    done(dve, dve.scalar_tensor_tensor(out=eidx[:, :], in0=key_f[:, i, 0, :], scalar=float(NKEYS),
                                                       in1=key_f[:, i, 1, :], op0=ALU.mult, op1=ALU.add), s_dv)
                dve.wait_ge(s_ge, tally[s_gd.name])
                done(dve, dve.tensor_reduce(gsum[:, :], gt, AX, ALU.add), s_dv)
                done(dve, dve.reciprocal(gsum[:, :], gsum[:, :]), s_dv)
                done(dve, dve.tensor_tensor(gt, gt, gsum[:, :].unsqueeze(2).to_broadcast([P, PH, TOPK]),
                                            ALU.mult), s_idx)

            emptied(dve, ("h2T", KD - 1))
            for k in range(KD):
                dve.wait_ge(s_hlo, k + 1)
            for tile in range(NT - GT):
                decode(tile + GT)
                if tile == NT - GT - 1:
                    decode(0)
                ps = taken(dve, ("cols", tile))
                dve.tensor_copy(cols[:, :, tile * P:tile * P + P], ps[:, 0:3 * P].rearrange("p (a b) -> p a b", b=P))\
                   .then_inc(freeing(("cols", tile)), 1)
                emptied(dve, ("cols", tile))

                def hot_first(tb, parity, i, slot):
                    for b in range(GB // 4):
                        B = tb * (GB // 4) + b
                        after(dve, s_gm, B - 1)
                        for tok in range(4):
                            n = tb * GB + 4 * b + tok
                            dve.tensor_scalar(hot_i[:, b % 2, tok, :], iota_k[:, :], cols[:, 0, bass.ds(n, 1)],
                                              cols[:, 2, bass.ds(n, 1)], ALU.is_equal, ALU.mult)
                        dve.tensor_tensor(hot_j[:, b % 2, :, :], iota_k[:, :].unsqueeze(1).to_broadcast([P, 4, P]),
                                          cols[:, 1, bass.ds(tb * GB + 4 * b, 4)].unsqueeze(2)
                                          .to_broadcast([P, 4, P]), ALU.is_equal).then_inc(s_hot, 1)

                gate_blocks(dve, tile, hot_first)
            done(dve, dve.memset(y0[:, :], 0.0), s_dv)
            dve.wait_ge(s_gm, DT // 4)
            for parity in range(2):
                dve.wait_ge(s_gst[parity], 16 * (DT // GB // 2))

            def weigh(i, c, late):
                dve.wait_ge(s_g[(c // 4) % 2], 16 * (over(i, c, 8) + 1))
                if late:
                    dve.wait_ge(s_al[c // 4], 2 * (i - c) - 2 * MAIN + 16)
                else:
                    dve.wait_ge(s_gelu, i + SPILL + 1)
                dve.tensor_tensor(w_f[:, :].rearrange("p (b t) -> p b t", t=GB),
                                  a_act[:, c, :].rearrange("p (b t) -> p b t", t=GB),
                                  g_in[:, (c // 4) % 2, :, c % 4, :], ALU.mult).then_inc(s_pw, 1)
                dve.wait_ge(s_pw, i + 1)
                after(dve, s_yv, i - 1)
                dve.tensor_copy(w_hi[:, c % 2, :], w_f[:, :]).then_inc(s_whi, 1)
                dve.wait_ge(s_whi, i + 1)
                dve.tensor_tensor(w_lo[:, c % 2, :], w_f[:, :], w_hi[:, c % 2, :].bitcast(f32), ALU.subtract)\
                   .then_inc(s_w, 1)
                dve.wait_ge(s_w, i + 1)

            def row_sum(n, c):
                q = slice(c % 2, c % 2 + 1)
                dve.wait_ge(s_dgelu, n + 1)
                dve.tensor_tensor(wgt[:, q], act_g[:, q], gate[:, 0, bass.ds(n, 1)], ALU.mult).then_inc(s_wgt, 1)
                dve.wait_ge(s_wgt, n + 1)
                after(dve, s_acc, n)
                place = place_of(n, c)
                dve.wait_ge(s_got[2 * place + 1], 16 * (over(n, c, RING) + 1))
                dve.scalar_tensor_tensor(out=y0[:, :], in0=rows[2 * place + 1][:, :], scalar=wgt[:, q], in1=y0[:, :],
                                         op0=ALU.mult, op1=ALU.add).then_inc(s_acc, 1)

            def chunk(i, c, late, numbers):
                weigh(i, c, late)
                dve.wait_ge(s_vhi, i + 1)
                dve.tensor_tensor(v_lo[:, c % 2, :], v_raw[:, c % 2, :], v_hi[:, c % 2, :].bitcast(f32), ALU.subtract)\
                   .then_inc(s_vlo, 1)
                for n, g in numbers:
                    after(dve, s_dot, n)
                    place = place_of(n, g)
                    dve.wait_ge(s_got[2 * place], 16 * (over(n, g, RING) + 1))
                    dve.scalar_tensor_tensor(out=junk[:, :], in0=rows[2 * place][:, :], scalar=1.0, in1=h2[:, 0, :],
                                             op0=ALU.mult, op1=ALU.mult, accum_out=dots[:, g % 2:g % 2 + 1])\
                       .then_inc(s_dot, 1)
                    if not isinstance(n, int) or n:
                        row_sum(n - 1, g - 1 if g else 11)
                    if isinstance(n, int) and n == PH * TOPK - 1:
                        row_sum(n, g)

            last_y = rows[1][:, 0:512], rows[1][:, 512:1024]

            def mean_squares(n, lo, hi):
                r = slice(2 * NT + lo, 2 * NT + hi)
                dve.wait_ge(s_f2, (NT - GT) * n + 1)
                dve.tensor_scalar(ss[:, r], ss[:, r], 1.0 / D, EPS, ALU.mult, ALU.add).then_inc(s_fm, 1)

            def last_norm(n, lo, hi):
                r = slice(2 * NT + lo, 2 * NT + hi)
                dve.wait_ge(s_fs, n + 1)
                done(dve, dve.reciprocal(rstd[:, r], rstd[:, r]), s_dv)
                dve.wait_ge(s_fin, 16)
                for i in range(lo, hi):
                    dve.scalar_tensor_tensor(out=x_sb[:, i, :], in0=x_sb[:, i, :],
                                             scalar=rstd[:, 2 * NT + i:2 * NT + i + 1],
                                             in1=fin_row[:, :], op0=ALU.mult, op1=ALU.mult).then_inc(s_res, 1)

            def chunk_and_tile(m, c, late, numbers):
                if isinstance(m, int) and m == NCHUNK - AHEAD:
                    dve.wait_ge(s_acc, PH * TOPK)
                    done(dve, dve.tensor_tensor(y0[:, :], y0[:, :], g2_row[:, :], ALU.mult), s_dv)
                    dve.tensor_tensor(x_sb[:, 0, :], x_sb[:, 0, :], y0[:, :], ALU.add).then_inc(s_x2, 1)
                chunk(m, c, late, numbers)
                if isinstance(m, int) and m == NCHUNK - AHEAD + 2:
                    mean_squares(0, 0, GT)
                if isinstance(m, int) and m == NCHUNK - AHEAD + 5:
                    last_norm(0, 0, GT)

            chunk_loop(dve, chunk_and_tile)

            dve.wait_ge(s_yv, NCHUNK)
            for i in range(GT, NT):
                for half in range(2):
                    part = slice(512 * half, 512 * half + 512)
                    done(dve, dve.tensor_tensor(last_y[half], y_bank[i - GT][half][:, :], g2_row[:, part],
                                                ALU.mult), s_dv)
                    ins = dve.tensor_tensor(x_sb[:, i, part], x_sb[:, i, part], last_y[half], ALU.add)
                    ins.then_inc(s_x2, 1)
            mean_squares(1, GT, NT)
            last_norm(1, GT, NT)


def kernel(**inputs):
    import concourse.bacc as bacc
    from concourse.bass_utils import run_bass_kernel_spmd as run

    a = {n: np.asarray(v) for n, v in inputs.items()}
    qa, ka, va, qb, kb, vb, qc, kc, vc = np.split(
        np.arange(a["w_in"].shape[2]), np.cumsum([256, 256, 256, 384, 384, 384, 384, 128]))
    qc = qc.reshape(2, CG, HD).transpose(1, 0, 2).reshape(-1)
    order = np.concatenate([qa, ka, qb, kb, qc, kc, va, vb, vc])
    w_in = a["w_in"][0][:, order].reshape(KD, P, IN_TILES, P).transpose(2, 1, 0, 3).reshape(IN_TILES, P, D)
    w_out = a["w_out"][0].reshape(NHEADS, HD, D)[[head[-1] for head in head_plan()]].reshape(D, D)
    wq = a["peer_wq"][0].reshape(KD, P, 2 * PH, P).transpose(2, 1, 0, 3).reshape(2 * PH, P, D)
    data = {
        "x": a["x"], "c_col": a["c"].reshape(KD, P).T, "norm1_col": a["norm1_g"].reshape(KD, P).T,
        "w_ada": a["w_ada"][0], "b_ada": a["b_ada"], "w_in": w_in, "w_out": w_out,
        "lam_vecs": np.concatenate([a[n][0] for n in ("lam_q1", "lam_k1", "lam_q2", "lam_k2")]),
        "subln_row": a["subln_g"][0], "sinks_row": a["sinks"][0], "norm2_row": a["norm2_g"][0], "wq": wq,
        "keys_t": a["peer_keys"][0].transpose(3, 0, 1, 2).reshape(P, 2 * PH, NKEYS),
        "peer_u": a["peer_u"][0], "peer_v": a["peer_v"][0],
        "u_t": a["peer_u"][0].reshape(NCHUNK, P, KD, P).transpose(0, 3, 2, 1).reshape(NCHUNK, P, D),
        "final_row": a["final_g"],
    }
    nc = bacc.Bacc("TRN2", target_bir_lowering=False, num_devices=1)
    arrays, args = {}, []
    for name, v in data.items():
        v = np.ascontiguousarray(v)
        arrays["in_" + name] = v
        args.append(nc.dram_tensor("in_" + name, v.shape, mybir.dt.from_np(v.dtype), kind="ExternalInput").ap())
    args.append(nc.dram_tensor("out_0", (1, S, D), mybir.dt.float32, kind="ExternalOutput").ap())
    peer_block_kernel(nc, *args)
    return run(nc, [arrays], core_ids=[0]).results[0]["out_0"]
```
